# Optimizing a Trainium2 kernel written in Bass

```python
import math
import jax, jax.numpy as jnp
from jax import lax
import numpy as np

D_MODEL = 1024
BATCH = 1
SEQ = 256
DEPTH = 2

CHUNK = 64
HEAD_DIM = 64
N_Q_HEADS = 8
N_KV_HEADS = 2
ATTN_WIDTH = N_Q_HEADS * HEAD_DIM
KV_WIDTH = N_KV_HEADS * HEAD_DIM
WINDOW = 128
WINDOW_CHUNKS = WINDOW // CHUNK
ROPE_DIM = HEAD_DIM // 4
ROPE_THETA = 500000.0
CONV_WIDTH = D_MODEL // 2
CONV_KERNEL = 31
SSM_WIDTH = D_MODEL // 2
SSM_GROUP = 16
SSM_GROUPS = SSM_WIDTH // SSM_GROUP
SSM_STATE = 64
N_BRANCH = 3
D_FF = -(-8 * D_MODEL // (3 * 256)) * 256
EPS = 1e-6
DT_MIN = 1e-3
DT_MAX = 1e-1
NEG_INF = -1e30

OFF_K = ATTN_WIDTH
OFF_V = OFF_K + KV_WIDTH
OFF_CA = OFF_V + KV_WIDTH
OFF_CB = OFF_CA + CONV_WIDTH
OFF_SU = OFF_CB + CONV_WIDTH
OFF_G = OFF_SU + SSM_WIDTH
IN_WIDTH = OFF_G + N_BRANCH * D_MODEL

kernel_name = "hybrid_swa_conformer_s5_adaln_trunk"

def rmsnorm(x, g):
    xf = x.astype(jnp.float32)
    y = xf * lax.rsqrt(jnp.mean(xf * xf, axis=-1, keepdims=True) + EPS)
    return (y * g.astype(jnp.float32)).astype(x.dtype)

def layernorm(x, g, b):
    xf = x.astype(jnp.float32)
    mu = jnp.mean(xf, axis=-1, keepdims=True)
    xc = xf - mu
    var = jnp.mean(xc * xc, axis=-1, keepdims=True)
    y = xc * lax.rsqrt(var + EPS) * g.astype(jnp.float32) + b.astype(jnp.float32)
    return y.astype(x.dtype)

def rope_tables(positions):
    inv = ROPE_THETA ** (-jnp.arange(0, ROPE_DIM, 2, dtype=jnp.float32) / ROPE_DIM)
    ang = positions.astype(jnp.float32)[..., None] * inv
    return jnp.cos(ang), jnp.sin(ang)

def apply_partial_rope(t, cos, sin):
    half = ROPE_DIM // 2
    tf = t.astype(jnp.float32)
    t1 = tf[..., :half]
    t2 = tf[..., half:ROPE_DIM]
    cc = cos[:, :, None, :]
    ss = sin[:, :, None, :]
    out = jnp.concatenate([t1 * cc - t2 * ss, t2 * cc + t1 * ss, tf[..., ROPE_DIM:]], axis=-1)
    return out.astype(t.dtype)

def sliding_window_attention(q, k, v, sinks):
    bsz, s = q.shape[0], q.shape[1]
    nc = s // CHUNK
    rep = N_Q_HEADS // N_KV_HEADS
    qc = q.astype(jnp.float32).reshape(bsz, nc, CHUNK, N_KV_HEADS, rep, HEAD_DIM)
    pad = (WINDOW_CHUNKS - 1) * CHUNK

    def band(t):
        tp = jnp.pad(t.astype(jnp.float32), ((0, 0), (pad, 0), (0, 0), (0, 0)))
        tcb = tp.reshape(bsz, nc + WINDOW_CHUNKS - 1, CHUNK, N_KV_HEADS, HEAD_DIM)
        return jnp.concatenate([tcb[:, j:j + nc] for j in range(WINDOW_CHUNKS)], axis=2)

    kb = band(k)
    vb = band(v)
    scores = jnp.einsum('bcqgrd,bckgd->bgrcqk', qc, kb) * (HEAD_DIM ** -0.5)
    slot_chunk = jnp.arange(WINDOW)[None, :] // CHUNK
    valid = (jnp.arange(nc)[:, None] + slot_chunk - (WINDOW_CHUNKS - 1)) >= 0
    scores = jnp.where(valid[None, None, None, :, None, :], scores, NEG_INF)
    sink = sinks.astype(jnp.float32).reshape(N_KV_HEADS, rep)[None, :, :, None, None, None]
    sink = jnp.broadcast_to(sink, scores.shape[:-1] + (1,))
    probs = jax.nn.softmax(jnp.concatenate([scores, sink], axis=-1), axis=-1)[..., :WINDOW]
    out = jnp.einsum('bgrcqk,bckgd->bcqgrd', probs, vb)
    return out.reshape(bsz, s, ATTN_WIDTH).astype(q.dtype)

def conformer_conv(a, b, w_dw, b_dw, ln_g, ln_b, w_pw):
    u = a * jax.nn.sigmoid(b)
    y = lax.conv_general_dilated(
        u, w_dw[:, None, :].astype(u.dtype), window_strides=(1,),
        padding=[(CONV_KERNEL - 1, 0)],
        dimension_numbers=('NWC', 'WIO', 'NWC'),
        feature_group_count=CONV_WIDTH) + b_dw
    y = jax.nn.silu(layernorm(y, ln_g, ln_b))
    return y @ w_pw

def s5_ssm(u, a_re, a_im, log_dt, b_re, b_im, c_re, c_im, d_skip, w_glu_a, w_glu_b):
    bsz, s = u.shape[0], u.shape[1]
    uf = u.astype(jnp.float32).reshape(bsz, s, SSM_GROUPS, SSM_GROUP)
    dt = jnp.exp(log_dt.astype(jnp.float32))[:, None]
    ar = a_re.astype(jnp.float32)
    ai = a_im.astype(jnp.float32)
    mag = jnp.exp(dt * ar)
    abar_re = mag * jnp.cos(dt * ai)
    abar_im = mag * jnp.sin(dt * ai)
    num_re = abar_re - 1.0
    num_im = abar_im
    den = ar * ar + ai * ai
    f_re = (num_re * ar + num_im * ai) / den
    f_im = (num_im * ar - num_re * ai) / den
    br = b_re.astype(jnp.float32)
    bi = b_im.astype(jnp.float32)
    bb_re = f_re[..., None] * br - f_im[..., None] * bi
    bb_im = f_re[..., None] * bi + f_im[..., None] * br
    bu_re = jnp.einsum('bsgi,gpi->bsgp', uf, bb_re)
    bu_im = jnp.einsum('bsgi,gpi->bsgp', uf, bb_im)
    at_re = jnp.broadcast_to(abar_re[None, None], (1, s, SSM_GROUPS, SSM_STATE))
    at_im = jnp.broadcast_to(abar_im[None, None], (1, s, SSM_GROUPS, SSM_STATE))

    def combine(left, right):
        alr, ali, blr, bli = left
        arr, ari, brr, bri = right
        return (arr * alr - ari * ali,
                arr * ali + ari * alr,
                arr * blr - ari * bli + brr,
                arr * bli + ari * blr + bri)

    _, _, h_re, h_im = lax.associative_scan(combine, (at_re, at_im, bu_re, bu_im), axis=1)
    y = (jnp.einsum('bsgp,gop->bsgo', h_re, c_re.astype(jnp.float32))
         - jnp.einsum('bsgp,gop->bsgo', h_im, c_im.astype(jnp.float32)))
    y = y.reshape(bsz, s, SSM_WIDTH) + d_skip.astype(jnp.float32) * u.astype(jnp.float32)
    y = y.astype(u.dtype)
    return (y @ w_glu_a) * jax.nn.sigmoid(y @ w_glu_b)

def setup_inputs(seed: int = 0) -> dict:
    key = jax.random.key(seed)
    ks = jax.random.split(key, 32)

    def nrm(k, shape, scale):
        return jax.random.normal(k, shape, jnp.float32) * scale

    L, D = DEPTH, D_MODEL
    x = nrm(ks[0], (BATCH, SEQ, D), 1.0)
    c = nrm(ks[1], (BATCH, D), 1.0)
    offsets = jax.random.randint(ks[2], (BATCH, 1), 0, 8192, dtype=jnp.int32)
    positions = offsets + jnp.arange(SEQ, dtype=jnp.int32)[None, :]
    n_idx = jnp.arange(SSM_STATE, dtype=jnp.float32)
    log_dt = jax.random.uniform(ks[3], (L, SSM_GROUPS), jnp.float32, math.log(DT_MIN), math.log(DT_MAX))
    return {
        "x": x,
        "c": c,
        "positions": positions,
        "w_mod": nrm(ks[4], (L, D, 6 * D), 0.5 * D ** -0.5),
        "b_mod": nrm(ks[5], (L, 6 * D), 0.02),
        "norm1_g": 1.0 + nrm(ks[6], (L, D), 0.02),
        "w_in": nrm(ks[7], (L, D, IN_WIDTH), D ** -0.5),
        "attn_sinks": nrm(ks[8], (L, N_Q_HEADS), 1.0),
        "w_attn_o": nrm(ks[9], (L, ATTN_WIDTH, D), ATTN_WIDTH ** -0.5),
        "conv_dw_w": nrm(ks[10], (L, CONV_KERNEL, CONV_WIDTH), CONV_KERNEL ** -0.5),
        "conv_dw_b": nrm(ks[11], (L, CONV_WIDTH), 0.02),
        "conv_ln_g": 1.0 + nrm(ks[12], (L, CONV_WIDTH), 0.02),
        "conv_ln_b": nrm(ks[13], (L, CONV_WIDTH), 0.02),
        "conv_pw_w": nrm(ks[14], (L, CONV_WIDTH, D), CONV_WIDTH ** -0.5),
        "ssm_a_re": -0.5 + nrm(ks[15], (L, SSM_GROUPS, SSM_STATE), 0.01),
        "ssm_a_im": jnp.pi * n_idx[None, None, :] + nrm(ks[16], (L, SSM_GROUPS, SSM_STATE), 0.01),
        "ssm_log_dt": log_dt,
        "ssm_b_re": nrm(ks[17], (L, SSM_GROUPS, SSM_STATE, SSM_GROUP), (2 * SSM_GROUP) ** -0.5),
        "ssm_b_im": nrm(ks[18], (L, SSM_GROUPS, SSM_STATE, SSM_GROUP), (2 * SSM_GROUP) ** -0.5),
        "ssm_c_re": nrm(ks[19], (L, SSM_GROUPS, SSM_GROUP, SSM_STATE), (2 * SSM_STATE) ** -0.5),
        "ssm_c_im": nrm(ks[20], (L, SSM_GROUPS, SSM_GROUP, SSM_STATE), (2 * SSM_STATE) ** -0.5),
        "ssm_d": nrm(ks[21], (L, SSM_WIDTH), 0.5),
        "ssm_glu_a": nrm(ks[22], (L, SSM_WIDTH, D), SSM_WIDTH ** -0.5),
        "ssm_glu_b": nrm(ks[23], (L, SSM_WIDTH, D), SSM_WIDTH ** -0.5),
        "w_out": nrm(ks[24], (L, D, D), D ** -0.5),
        "norm2_g": 1.0 + nrm(ks[25], (L, D), 0.02),
        "w_ffn_in": nrm(ks[26], (L, D, 2 * D_FF), D ** -0.5),
        "w_ffn_out": nrm(ks[27], (L, D_FF, D), D_FF ** -0.5),
        "final_norm_g": 1.0 + nrm(ks[28], (D,), 0.02),
    }

def reference(x, c, positions, w_mod, b_mod, norm1_g, w_in, attn_sinks, w_attn_o,
              conv_dw_w, conv_dw_b, conv_ln_g, conv_ln_b, conv_pw_w,
              ssm_a_re, ssm_a_im, ssm_log_dt, ssm_b_re, ssm_b_im, ssm_c_re, ssm_c_im, ssm_d,
              ssm_glu_a, ssm_glu_b, w_out, norm2_g, w_ffn_in, w_ffn_out, final_norm_g):
    bsz, s, _ = x.shape
    cos, sin = rope_tables(positions)
    c_act = jax.nn.silu(c)
    for l in range(DEPTH):
        mod = (c_act @ w_mod[l] + b_mod[l])[:, None, :]
        sh1, sc1, g1, sh2, sc2, g2 = jnp.split(mod, 6, axis=-1)

        h = rmsnorm(x, norm1_g[l]) * (1.0 + sc1) + sh1
        proj = h @ w_in[l]
        q, k, v, ca, cb, su, gates = jnp.split(
            proj, [OFF_K, OFF_V, OFF_CA, OFF_CB, OFF_SU, OFF_G], axis=-1)
        q = apply_partial_rope(q.reshape(bsz, s, N_Q_HEADS, HEAD_DIM), cos, sin)
        k = apply_partial_rope(k.reshape(bsz, s, N_KV_HEADS, HEAD_DIM), cos, sin)
        v = v.reshape(bsz, s, N_KV_HEADS, HEAD_DIM)
        y_attn = sliding_window_attention(q, k, v, attn_sinks[l]) @ w_attn_o[l]
        y_conv = conformer_conv(ca, cb, conv_dw_w[l], conv_dw_b[l], conv_ln_g[l], conv_ln_b[l], conv_pw_w[l])
        y_ssm = s5_ssm(su, ssm_a_re[l], ssm_a_im[l], ssm_log_dt[l], ssm_b_re[l], ssm_b_im[l],
                       ssm_c_re[l], ssm_c_im[l], ssm_d[l], ssm_glu_a[l], ssm_glu_b[l])
        gate_a, gate_c, gate_s = jnp.split(jax.nn.sigmoid(gates), N_BRANCH, axis=-1)
        mixed = gate_a * y_attn + gate_c * y_conv + gate_s * y_ssm
        x = x + g1 * (mixed @ w_out[l])

        h2 = rmsnorm(x, norm2_g[l]) * (1.0 + sc2) + sh2
        gu = h2 @ w_ffn_in[l]
        f_gate, f_up = jnp.split(gu, 2, axis=-1)
        x = x + g2 * ((jax.nn.silu(f_gate) * f_up) @ w_ffn_out[l])
    return rmsnorm(x, final_norm_g)


_drawn_inputs = setup_inputs


def setup_inputs(seed=0):
    import zlib

    import numpy as np

    out = dict(_drawn_inputs(seed))
    spreads = {}
    factors = {'norm1_g': 8.0,
     'attn_sinks': 8.0,
     'conv_dw_b': 8.0,
     'conv_ln_g': 8.0,
     'conv_ln_b': 8.0,
     'ssm_a_re': 64.0,
     'ssm_a_im': 48.72,
     'ssm_log_dt': 56.576,
     'ssm_b_re': 64.0,
     'ssm_b_im': 64.0,
     'ssm_c_re': 64.0,
     'ssm_c_im': 64.0,
     'ssm_glu_b': 3.305,
     'norm2_g': 6.314,
     'final_norm_g': 7.471}
    for name, (base, spread) in spreads.items():
        noise = np.random.default_rng([zlib.crc32(name.encode()), seed]).standard_normal(out[name].shape)
        drawn = base * np.exp(spread * noise) if base else spread * noise
        out[name] = __import__('jax').numpy.asarray(drawn.astype(out[name].dtype))
    for name, factor in factors.items():
        out[name] = (out[name] * factor).astype(out[name].dtype)
    return out
```

```python
from contextlib import ExitStack

import numpy as np
import concourse.bass as bass
from concourse import mybir

ALU = mybir.AluOpType
ACT = mybir.ActivationFunctionType
F32 = mybir.dt.float32
F32R = mybir.dt.float32r
I32 = mybir.dt.int32
AX_X = mybir.AxisListType.X

P = 128
D = 1024
T = 256
DEPTH = 2
DK = D // P
HEAD = 64
NQ = 8
NKV = 2
CHUNK = 64
KEYS = 128
TAPS = 31
PAD = TAPS - 1
CW = 512
CT = CW // P
ST = 16
GROUP = 16
DFF = 2816
FK = DFF // P
EPS = 1e-6
NEG = -1e30
ROPE_DIM = 16
THETA = 500000.0
OFF_K, OFF_V, OFF_CA, OFF_CB, OFF_SU, OFF_G = 512, 640, 768, 1280, 1792, 2304
BC = 256
MODC = 2048

ROUND = 12582912.0
TWO_PI = 6.283185307179586
PI_LOW = float(np.nextafter(np.float32(np.pi), np.float32(0)))
C1 = 6.28125
C2 = float(np.float32(np.round((TWO_PI - C1) * 2**22) / 2**22))
C3 = float(np.float32(TWO_PI - C1 - C2))

R_BMOD, R_N1, R_N2, R_DWB, R_LNG, R_LNB, R_D, R_ARE, R_AIM, R_FIN, R_C = 0, 48, 56, 64, 68, 72, 76, 80, 96, 112, 120
M_SH1, M_SC1, M_G1, M_SH2, M_SC2, M_G2 = 0, 8, 16, 24, 32, 40


def block_names():
    names = [("su", 0), ("su", 1), ("q", 0), ("q", 1), ("kv", 0), ("cb", 0), ("ca", 0), ("cb", 1), ("ca", 1)]
    names += [("ga", n) for n in range(4)] + [("ao", 0), ("ao", 1)]
    names += [("gc", n) for n in range(4)] + [("cp", 0), ("cp", 1)]
    names += [("gs", n) for n in range(4)] + [("glb", 0), ("gla", 0), ("glb", 1), ("gla", 1)]
    names += [("wo", n) for n in range(4)]
    for n in range(FK // 2):
        names += [("fg", n), ("fu", n)]
        if n:
            names += [("fo", n - 1)]
    return names + [("fo", FK // 2 - 1)]


NAMES = block_names()
NB = len(NAMES)
AT = {name: i for i, name in enumerate(NAMES)}
N_UNITS = {"kv": 2, "ao": 2, "cp": 2, "gla": 2, "glb": 2}
UNIT0 = [sum(N_UNITS.get(NAMES[j][0], 1) for j in range(i)) for i in range(NB + 1)]
BANK0 = [sum(N_UNITS.get(NAMES[j][0], 1) for j in range(i) if NAMES[j][0] != "fo") for i in range(NB + 1)]
UNITS, BANKS = UNIT0[NB], BANK0[NB]
NF = FK // 2

SSM_AT = {2: [0, 1], 3: [2, 3], 4: [4, 5], 5: [6, 7], 6: [8, 9], 7: [10], 8: [11], 17: [12], 18: [13], 19: [14], 20: [15]}
ROPE_AT = AT[("cb", 0)] + 1
ATTN_AT = {7: 0, 8: 1, 9: 2, 10: 3}
CONV_AT = {9 + n: (n // 4, n % 4) for n in range(8)}
CONV_NORM_AT = 17
MOD_AT = {5 + n: (1, n) for n in range(DK)} | {14 + n: (2, n) for n in range(DK)}
NEXT_MOD_AT = {AT[("fg", 1)] + 3 * n: (0, n) for n in range(DK)}
PREP_AT = AT[("fg", 1)]
BC_AT = {PREP_AT + 1 + 2 * n: n for n in range(4)}
TABLE_AT = {AT[("fg", 5 + n)]: n for n in range(4)}

N_LOADS = {"q": 4, "ao": 2}
N_RAW, N_HI, N_LO = 4, 3, 2
AHEAD = 2


def lo_engine(i):
    return "pool" if NAMES[i][0] not in ("wo", "fg", "fu", "fo") else "dve"


def mods_at(l, i):
    found = [(l, *MOD_AT[i])] if i in MOD_AT else []
    return found + ([(l + 1, *NEXT_MOD_AT[i])] if i in NEXT_MOD_AT and l + 1 < DEPTH else [])


def mod_ends_at(l, i):
    return [3 * m[0] + m[1] for m in mods_at(l, i) if m[2] == DK - 1] if i >= 0 else []


def used(mi):
    return (mi // NB) * UNITS + UNIT0[mi % NB + 1]


def plan_loads():
    items = [("mod", 0, 0, k) for k in range(DK)]
    for l in range(DEPTH):
        for i in range(NB):
            items += [("mod", *m) for m in mods_at(l, i)]
            items.append(("main", l, i))
    count, slot_of, landed, after = [0] * N_RAW, {}, {}, {}
    owner = [None] * N_RAW
    for n, item in enumerate(items):
        s = n % N_RAW
        count[s] += 16 * (N_LOADS.get(NAMES[item[2]][0], 1) if item[0] == "main" else 1)
        slot_of[item], landed[item], after[item] = s, count[s], owner[s]
        owner[s] = item
    return items, slot_of, landed, after


ITEMS, SLOT, LANDED, AFTER = plan_loads()
MOD_ITEMS = [x for x in ITEMS if x[0] == "mod"]
MOD_NO = {x: n for n, x in enumerate(MOD_ITEMS)}
LO_NO = {}
for _e in ("pool", "dve"):
    for _n, _m in enumerate([(l, i) for l in range(DEPTH) for i in range(NB) if lo_engine(i) == _e]):
        LO_NO[_m] = _n


UNIT_OF = [(l, i, n) for l in range(DEPTH) for i in range(NB) if NAMES[i][0] != "fo" for n in range(N_UNITS.get(NAMES[i][0], 1))]
N_ROWS = 13


class Steps:

    def __init__(self, sem):
        self.sem, self.n = sem, 0

    def __call__(self, ins):
        self.n += 1
        ins.then_inc(self.sem, 1)
        return self.n


def trunk(nc, A, out):
    with ExitStack() as ctx:
        def sb(name, shape, dt=F32):
            return ctx.enter_context(nc.sbuf_tensor(name, shape, dt))

        def sem(name):
            return ctx.enter_context(nc.semaphore(name))

        bank = [ctx.enter_context(nc.psum_tensor(f"bank{n}", [P, 512], F32)) for n in range(8)]
        b_mod, b_y = bank[2], bank[3]
        b_bu = [bank[4], bank[5]]
        b_s, b_t = bank[6], bank[7]

        raw = [sb(f"raw{n}", [P, 2048]) for n in range(N_RAW)]
        whi = [sb(f"whi{n}", [P, 2048], F32R) for n in range(N_HI)]
        wlo = [sb(f"wlo{n}", [P, 2048], F32R) for n in range(N_LO)]
        x = sb("x", [P, DK, T])
        h = sb("h", [P, DK, T])
        hhi = sb("hhi", [P, DK, T], F32R)
        hlo = sb("hlo", [P, DK, T], F32R)
        gate = sb("gate", [P, DK, T])
        bhi = sb("bhi", [P, 4, T], F32R)
        blo = sb("blo", [P, 4, T], F32R)
        ctab = sb("ctab", [P, ST, T])
        stab = sb("stab", [P, ST, T])
        m = sb("m", [P, 4, T])
        prod = [sb(f"prod{n}", [P, 4, T]) for n in range(2)]
        u_ssm = sb("u_ssm", [P, CT, T])
        ys = u_ssm
        uc = sb("uc", [P, CT, PAD + T])
        yc = sb("yc", [P, CT, T])
        qT = h[:, 0:4, :]
        kT = sb("kT", [P, T])
        vv = sb("vv", [P, 3, P])
        rtmp = m[:, 0:2, :]
        pr = h[:, 4:6, :].rearrange("p a b -> p (a b)").rearrange("p (t k) -> p t k", t=4)
        pT = h[:, 6:8, :].rearrange("p a b -> p (a b)").rearrange("p (t k) -> p t k", t=4)
        tmp = sb("tmp", [P, 2, T])
        rinv = sb("rinv", [P, T])
        mean = rinv
        modrow = sb("modrow", [P, 512])
        cosr = sb("cosr", [P, T])
        sinr = sb("sinr", [P, T])
        iota = sb("iota", [P, T])
        ident = sb("ident", [P, P])
        ones = sb("ones", [P, P])
        rot = sb("rot", [P, P])
        consts = sb("consts", [P, 16])
        rows = prod[1][:, 0, 0:P]
        ldt = sb("ldt", [ST, 2])
        ldtr = prod[1][0:ST, 0, P:2 * P]
        taps = prod[0][0:TAPS, 0:2, :].rearrange("p a b -> p (a b)")
        vec = [sb(f"vec{l}", [P, P]) for l in range(DEPTH)]
        ldv = [sb(f"ldv{l}", [P, ST]) for l in range(DEPTH)]
        tapv = [sb(f"tapv{l}", [P, CT, TAPS]) for l in range(DEPTH)]
        sink = sb("sink", [P, DEPTH, NQ])
        modv = sb("modv", [P, 48])
        scale1 = sb("scale1", [P, DK])
        scale2 = sb("scale2", [P, DK])
        cact = sb("cact", [P, DK])
        cact32 = sb("cact32", [P, DK, 32])
        small = sb("small", [P, 24, ST])
        bn = yc[:, 0:2, :].rearrange("p a (s i) -> p a s i", i=GROUP)
        cn = yc[:, 2:4, :].rearrange("p a (s n) -> p a s n", n=HEAD)
        uc_flat = uc[:, :, :].rearrange("p c t -> p (c t)")
        bt = uc_flat[:, 0:512].rearrange("p (a s i) -> p a s i", a=2, i=GROUP)
        bsrc = uc_flat[:, 512:1024].rearrange("p (s i) -> p s i", i=2 * GROUP)
        csrc = prod[1][:, 2:4, :].rearrange("p a b -> p (a b)").rearrange("p (c n) -> p c n", c=CT)
        bl = sb("bl", [P, 2, CT, P])
        cl = sb("cl", [P, 3, CT, P])
        mx = sb("mx", [P, 4])
        nmx = sb("nmx", [P, 4])
        den = sb("den", [P, 4])
        esink = sb("esink", [P, 4])
        rden = sb("rden", [P, 4])
        posi = modrow[:, 0:T].bitcast(I32)

        s_const, s_const2, s_bc, s_x = sem("const_landed"), sem("late_const_landed"), sem("bc_landed"), sem("x_landed")
        s_rows = [sem(f"rows_landed{l}") for l in range(DEPTH)]
        s_land = [sem(f"raw_landed{n}") for n in range(N_RAW)]
        s_hi, s_unit, s_modused = sem("hi_ready"), sem("unit_ready"), sem("mod_weights_used")
        s_lo = {"pool": sem("lo_ready_pool"), "dve": sem("lo_ready_dve")}
        s_dve, s_act = sem("dve_step"), sem("act_step")
        s_out = sem("out_stored")
        ldt_spread, vec_tr, vec_cp, x_tr, x_cp, silu_c, c_ready = (
            sem(n) for n in "ldt_spread vec_tr vec_cp x_tr x_cp silu_c c_ready".split())
        mod_row, mod_tr, mod_ready = (
            sem(n) for n in "mod_row mod_tr mod_ready".split())
        sq_ready, stat_ready, rms_ready, h_ready, hhi_ready, hlo_ready = (
            sem(n) for n in "sq_ready stat_ready rms_ready h_ready hhi_ready hlo_ready".split())
        u_ready, bu_ready, bu_used, prod_ready, y_ready, y_used, ys_hi, ys_lo = (
            sem(n) for n in "u_ready bu_ready bu_used prod_ready y_ready y_used ys_hi ys_lo".split())
        qk_ready, rot_ready, rope_ready, v_ready = (
            sem(n) for n in "qk_ready rot_ready rope_ready v_ready".split())
        sc_ready, mx_ready, ex_ready, pr_ready, pt_ready, pt_copied, pv_ready, at_hi, at_lo = (
            sem(n) for n in "sc_ready mx_ready ex_ready pr_ready pt_ready pt_copied pv_ready at_hi at_lo".split())
        sigb_ready, uc_ready, conv_ready, csum_ready, mean_ready, cent_ready, csq_ready, cvar_ready, cstd_ready, cnorm_ready, csilu_ready, c_hi, c_lo = (
            sem(n) for n in "sigb_ready uc_ready conv_ready csum_ready mean_ready cent_ready csq_ready cvar_ready cstd_ready cnorm_ready csilu_ready c_hi c_lo".split())
        gate_ready, ao_read, cp_read, glsig_ready, gl_read, gl_done = (
            sem(n) for n in "gate_ready ao_read cp_read glsig_ready gl_read gl_done".split())
        x_mid, x_next, silu_ready, act_ready, act_hi, act_lo, ffn_sum = (
            sem(n) for n in "x_mid x_next silu_ready act_ready act_hi act_lo ffn_sum".split())
        prep_exp, prep_ang, prep_mag, prep_arg, prep_sin, bc_src, bc_tr, bc_cp = (
            sem(n) for n in "prep_exp prep_ang prep_mag prep_arg prep_sin bc_src bc_tr bc_cp".split())
        rope_ang, rope_sin, rope_tab, tab_ang, tab_sin, tab_ready = (
            sem(n) for n in "rope_ang rope_sin rope_tab tab_ang tab_sin tab_ready".split())
        fin_ready, fin_tr, fin_cp = (
            sem(n) for n in "fin_ready fin_tr fin_cp".split())

        w_in, w_ffn_in = A["w_in"], A["w_ffn_in"]

        def by_k(w, l):
            return w[l].rearrange("(k p) n -> p k n", p=P)

        block = ctx.enter_context(nc.Block())

        @block.sync
        def _(sp):
            sp.dma_start(ident[:, :], A["c_ident"]).then_inc(s_const, 16)
            sp.dma_start(consts[:, :], A["c_small"]).then_inc(s_const, 16)

            def small_vectors(l):
                if l:
                    sp.wait_ge(vec_tr, 1)
                for r0, n, name in ((R_BMOD, 48, "b_mod"), (R_N1, 8, "norm1_g"), (R_N2, 8, "norm2_g"), (R_DWB, 4, "conv_dw_b"),
                                    (R_LNG, 4, "conv_ln_g"), (R_LNB, 4, "conv_ln_b"), (R_D, 4, "ssm_d")):
                    sp.dma_start(rows[r0:r0 + n, :], A[name][l].rearrange("(r c) -> r c", c=P)).then_inc(s_rows[l], 16)
                for r0, name in ((R_ARE, "ssm_a_re"), (R_AIM, "ssm_a_im")):
                    sp.dma_start(rows[r0:r0 + ST, :], A[name][l].rearrange("(s g) n -> s (g n)", g=2)).then_inc(s_rows[l], 16)
                sp.dma_start(rows[R_FIN:R_FIN + DK, :], A["final_norm_g"].rearrange("(r c) -> r c", c=P)).then_inc(s_rows[l], 16)
                sp.dma_start(rows[R_C:R_C + DK, :], A["c"].rearrange("b (r c) -> (b r) c", c=P)).then_inc(s_rows[l], 16)
                sp.dma_start(ldt[:, :], A["ssm_log_dt"][l].rearrange("(s g) -> s g", g=2)).then_inc(s_rows[l], 16)
                sp.dma_start(taps, A["conv_dw_w"][l]).then_inc(s_rows[l], 16)

            def b_and_c(l):
                for c, name in enumerate(("ssm_b_re", "ssm_b_im")):
                    sp.dma_start(bn[:, c], A[name][l].rearrange("g n i -> (g n) i").rearrange("(s p) i -> p s i", p=P)).then_inc(s_bc, 16)
                for c, name in enumerate(("ssm_c_re", "ssm_c_im")):
                    sp.dma_start(cn[:, c], A[name][l].rearrange("g o n -> (g o) n").rearrange("(s p) n -> p s n", p=P)).then_inc(s_bc, 16)

            def main(l, i, dst):
                kind, n = NAMES[i]
                k8 = dst.rearrange("p (k n) -> p k n", k=DK)
                k4 = dst.rearrange("p (k n) -> p k n", k=4)
                if kind in ("su", "ca", "cb", "ga", "gc", "gs", "kv"):
                    c0 = {"su": OFF_SU, "ca": OFF_CA, "cb": OFF_CB, "ga": OFF_G, "gc": OFF_G + D, "gs": OFF_G + 2 * D, "kv": OFF_K}[kind] + BC * n
                    return [(k8, by_k(w_in, l)[:, :, c0:c0 + BC])]
                if kind == "q":
                    return [(k8[:, :, c * P + g * HEAD:c * P + (g + 1) * HEAD],
                             by_k(w_in, l)[:, :, g * 256 + (2 * n + c) * HEAD:g * 256 + (2 * n + c + 1) * HEAD]) for c in range(2) for g in range(NKV)]
                if kind == "ao":
                    w = A["w_attn_o"][l].rearrange("(g t d) n -> g d t n", g=NKV, d=HEAD)
                    return [(k4[g * HEAD:(g + 1) * HEAD], w[g][:, :, n * 512:(n + 1) * 512]) for g in range(NKV)]
                if kind in ("cp", "gla", "glb"):
                    w = A[{"cp": "conv_pw_w", "gla": "ssm_glu_a", "glb": "ssm_glu_b"}[kind]]
                    return [(k4, by_k(w, l)[:, :, n * 512:(n + 1) * 512])]
                if kind == "wo":
                    return [(k8, by_k(A["w_out"], l)[:, :, n * BC:(n + 1) * BC])]
                if kind in ("fg", "fu"):
                    c0 = n * BC + (DFF if kind == "fu" else 0)
                    return [(k8, by_k(w_ffn_in, l)[:, :, c0:c0 + BC])]
                return [(dst.rearrange("p (k n) -> p k n", k=2), by_k(A["w_ffn_out"], l)[:, 2 * n:2 * n + 2, :])]

            small_vectors(0)
            for n, item in enumerate(ITEMS):
                if n == 2:
                    for j in range(2):
                        sp.dma_start(h[:, 4 * j:4 * j + 4, :].rearrange("p a b -> p (a b)"), A["x"][0, j * P:(j + 1) * P, :]).then_inc(s_x, 16)
                    b_and_c(0)
                    sp.dma_start(ones[:, :], A["c_ones"]).then_inc(s_const2, 16)
                    sp.dma_start(rot[:, :], A["c_rot"]).then_inc(s_const2, 16)
                    sp.dma_start(iota[:, :], A["c_iota"]).then_inc(s_const2, 16)
                    sp.dma_start(posi, A["positions"].to_broadcast([P, T])).then_inc(s_const2, 16)
                    sp.dma_start(sink[:, :, :], A["attn_sinks"].rearrange("(o l) q -> o l q", o=1).to_broadcast([P, DEPTH, NQ])).then_inc(s_const2, 16)
                    small_vectors(1)
                was = AFTER[item]
                if was and was[0] == "main":
                    e = lo_engine(was[2])
                    sp.wait_ge(s_lo[e], LO_NO[(was[1], was[2])] + 1)
                elif was:
                    sp.wait_ge(s_modused, MOD_NO[was] + 1)
                dst = raw[SLOT[item]][:, :]
                if item[0] == "mod":
                    _, l, ng, k = item
                    sp.dma_start(dst, A["w_mod"][l, k * P:(k + 1) * P, ng * MODC:(ng + 1) * MODC]).then_inc(s_land[SLOT[item]], 16)
                else:
                    for d, src in main(item[1], item[2], dst):
                        sp.dma_start(d, src).then_inc(s_land[SLOT[item]], 16)
                    if item[1] == 0 and DEPTH > 1 and item[2] == AT[("wo", 0)]:
                        sp.wait_ge(bc_src, 4)
                        b_and_c(1)
            for j in range(2):
                sp.wait_ge(fin_cp, 2 * j + 2)
                sp.dma_start(out[0, j * P:(j + 1) * P, :], h[:, 4 * j:4 * j + 4, :].rearrange("p a b -> p (a b)")).then_inc(s_out, 16)
            sp.wait_ge(s_out, 32)

        @block.tensor
        def _(pe):
            mm = nc.tensor.matmul

            def hi_lo(o, w_hi, w_lo, a_hi, a_lo, start, stop):
                mm(o, w_hi, a_hi, start=start, stop=False, skip_group_check=True)
                mm(o, w_hi, a_lo, start=False, stop=False, skip_group_check=True)
                return mm(o, w_lo, a_hi, start=False, stop=stop, skip_group_check=True)

            def unit_bank(l, i, n=0):
                b = l * BANKS + BANK0[i] + n
                if b >= 2:
                    pl, pi, pn = UNIT_OF[b - 2]
                    kind, kn = NAMES[pi]
                    done, value = {
                        "su": (u_ready, 2 * pl + kn + 1), "q": (qk_ready, 3 * pl + kn + 1),
                        "kv": (qk_ready, 3 * pl + 3) if pn == 0 else (v_ready, pl + 1),
                        "cb": (sigb_ready, 2 * pl + kn + 1), "ca": (uc_ready, 2 * pl + kn + 1),
                        "ga": (gate_ready, 12 * pl + kn + 1), "gc": (gate_ready, 12 * pl + 5 + kn), "gs": (gate_ready, 12 * pl + 9 + kn),
                        "ao": (ao_read, 4 * pl + 2 * kn + pn + 1), "cp": (cp_read, 4 * pl + 2 * kn + pn + 1),
                        "glb": (glsig_ready, 4 * pl + 2 * kn + pn + 1), "gla": (gl_read, 4 * pl + 2 * kn + pn + 1),
                        "wo": (x_mid, 4 * pl + kn + 1), "fg": (silu_ready, NF * pl + kn + 1), "fu": (act_ready, NF * pl + kn + 1),
                    }[kind]
                    pe.wait_ge(done, value)
                return bank[b % 2]

            def mod_block(l, ng, k):
                item = ("mod", l, ng, k)
                pe.wait_ge(s_land[SLOT[item]], LANDED[item])
                if MOD_NO[item] == 0:
                    pe.wait_ge(c_ready, 1)
                elif k == 0:
                    pe.wait_ge(mod_ready, MOD_NO[item] // DK)
                for q in range(4):
                    last = mm(b_mod[32 * q:32 * q + 32, :], cact32[:, k, :], raw[SLOT[item]][:, q * 512:(q + 1) * 512],
                              start=(k == 0), stop=(k == DK - 1), skip_group_check=True)
                last.then_inc(s_modused, 1)

            def mod_columns(n):
                pe.wait_ge(mod_row, n + 1)
                for j in range(4):
                    last = mm(b_mod[:, 4 * j:4 * j + 4], modrow[:, j * P:(j + 1) * P], consts[:, 0:4], start=(j == 0), stop=(j == 3), skip_group_check=True)
                last.then_inc(mod_tr, 1)

            def mean_square(n):
                if n == 0:
                    pe.wait_ge(s_const2, 16 * 5)
                elif n % 2:
                    pe.wait_ge(y_used, n + 1)
                elif n < 2 * DEPTH:
                    pe.wait_ge(bc_cp, 4 * (n // 2 + 1))
                for k in range(DK):
                    if k % 4 == 0:
                        pe.wait_ge(sq_ready, 2 * n + k // 4 + 1)
                    last = mm(b_y[:, 0:T], ones[:, :], h[:, k, :], start=(k == 0), stop=(k == DK - 1))
                last.then_inc(stat_ready, 1)

            def ssm_in(l, t):
                n = l * ST + t
                pe.wait_ge(u_ready, 2 * l + t // 8 + 1)
                if t == 0:
                    pe.wait_ge(bc_cp, 4 * (l + 1))
                if n >= 2:
                    pe.wait_ge(bu_used, n - 1)
                r = 32 * (t % 4)
                for c in range(2):
                    last = mm(b_bu[t % 2][:, c * T:(c + 1) * T], bl[r:r + 32, c, t // 4, :], u_ssm[r:r + 32, t // 4, :], start=True, stop=True)
                last.then_inc(bu_ready, 1)

            def ssm_out(l, t):
                n = l * ST + t
                pe.wait_ge(prod_ready, n + 1)
                if t % 8 == 0 and n:
                    pe.wait_ge(y_used, n // 8)
                if t == 0:
                    pe.wait_ge(rms_ready, 2 * l + 1)
                r = 32 * (t % 4)
                half = (t // 4) % 2
                for c, w in enumerate((0, 2, 2, 1)):
                    last = mm(b_y[r:r + 32, half * T:(half + 1) * T], cl[:, w, t // 4, r:r + 32], prod[t % 2][:, c, :],
                              start=(c == 0), stop=(c == 3), skip_group_check=True)
                last.then_inc(y_ready, 1)

            def rotate(l):
                pe.wait_ge(qk_ready, 3 * l + 3)
                for c in range(3):
                    o = (b_s, b_t, b_s)[c]
                    if c == 2:
                        pe.wait_ge(rope_ready, 3 * l + 1)
                    for j in range(2 if c < 2 else 1):
                        src = qT[:, 2 * c + j, :] if c < 2 else kT[:, :]
                        last = mm(o[:, j * T:(j + 1) * T], rot[:, :], src, start=(j == 0), stop=True, skip_group_check=True)
                    last.then_inc(rot_ready, 1)

            def scores(l, r):
                n = 4 * l + r
                j, g = divmod(r, 2)
                p = slice(g * HEAD, (g + 1) * HEAD)
                if r == 0:
                    pe.wait_ge(rope_ready, 3 * l + 3)
                else:
                    pe.wait_ge(ex_ready, n)
                for t in range(4):
                    o = b_s[:, t * KEYS:(t + 1) * KEYS]
                    if j == 0:
                        last = mm(o, qT[p, t, 0:P], kT[p, 0:P], start=(t == 0), stop=(t == 3), skip_group_check=True)
                    else:
                        for c in range(2):
                            last = mm(o[c * CHUNK:(c + 1) * CHUNK, :], qT[p, t, P + c * CHUNK:P + (c + 1) * CHUNK],
                                      kT[p, CHUNK * (c + 1):CHUNK * (c + 1) + KEYS], start=(t == 0), stop=(t == 3), skip_group_check=True)
                last.then_inc(sc_ready, 1)

            def probs_t(l, r):
                n = 4 * l + r
                pe.wait_ge(pr_ready, n + 1)
                if r == 0:
                    pe.wait_ge(rope_ready, 3 * l + 2)
                else:
                    pe.wait_ge(at_lo, n)
                for t in range(4):
                    last = nc.tensor.transpose(b_t[:, t * P:(t + 1) * P], pr[:, t, :], ident[:, :])
                last.then_inc(pt_ready, 1)

            def attend(l, r):
                n = 4 * l + r
                j, g = divmod(r, 2)
                p = slice(g * HEAD, (g + 1) * HEAD)
                pe.wait_ge(pt_copied, n + 1)
                if r == 0:
                    pe.wait_ge(v_ready, l + 1)
                o = b_t[p, :].rearrange("p (t q) -> p t q", t=4)
                if j == 0:
                    last = mm(o, vv[:, 0, p], pT[:, :, :], start=True, stop=True)
                else:
                    for c in range(2):
                        last = mm(o[:, :, c * CHUNK:(c + 1) * CHUNK], vv[:, 1 + c, p], pT[:, :, c * CHUNK:(c + 1) * CHUNK],
                                  start=(c == 0), stop=(c == 1), skip_group_check=True)
                last.then_inc(pv_ready, 1)

            def conv_stat(l, n):
                if n == 0:
                    pe.wait_ge(at_lo, 4 * (l + 1))
                pe.wait_ge(conv_ready if n == 0 else csq_ready, l + 1)
                src = yc[:, :, :] if n == 0 else uc[:, :, 0:T]
                for c in range(CT):
                    last = mm(b_t[:, n * T:(n + 1) * T], ones[:, :], src[:, c, :], start=(c == 0), stop=(c == CT - 1), skip_group_check=True)
                last.then_inc(csum_ready if n == 0 else cvar_ready, 1)

            def bc_transposes(l, n):
                pe.wait_ge(bc_src, 4 * l + n + 1)
                if n:
                    pe.wait_ge(bc_cp, 4 * l + n)
                else:
                    pe.wait_ge(rms_ready, 2 * l if l else 1)
                for c in range(CT):
                    src = bsrc[:, 4 * c:4 * c + 4, :].rearrange("p a b -> p (a b)") if n < 2 else csrc[:, c, :]
                    last = nc.tensor.transpose(b_y[:, c * P:(c + 1) * P], src, ident[:, :])
                last.then_inc(bc_tr, 1)

            def main_block(l, i, mid):
                kind, n = NAMES[i]
                mi = l * NB + i
                W, V = whi[mi % N_HI], wlo[mi % N_LO]
                pe.wait_ge(s_lo[lo_engine(i)], LO_NO[(l, i)] + 1)
                w8 = [w[:, :].rearrange("p (k n) -> p k n", k=DK) for w in (W, V)]
                w4 = [w[:, :].rearrange("p (k n) -> p k n", k=4) for w in (W, V)]
                if n == 0 and kind in ("su", "wo", "fg"):
                    pe.wait_ge(hlo_ready, 2 * (3 * l + {"su": 0, "wo": 1, "fg": 2}[kind]) + 2)
                if kind == "kv":
                    o = unit_bank(l, i)
                    for k in range(DK):
                        last = hi_lo(o[:, 0:T], w8[0][:, k, 0:P], w8[1][:, k, 0:P], hhi[:, k, :], hlo[:, k, :], k == 0, k == DK - 1)
                    last.then_inc(s_unit, 1)
                    mid()
                    o = unit_bank(l, i, 1)
                    for c in range(3):
                        t0 = CHUNK * c if c < 2 else P
                        for k in range(DK):
                            last = hi_lo(o[:, c * P:(c + 1) * P], hhi[:, k, t0:t0 + P], hlo[:, k, t0:t0 + P],
                                         w8[0][:, k, P:2 * P], w8[1][:, k, P:2 * P], k == 0, k == DK - 1)
                    last.then_inc(s_unit, 1)
                elif kind in ("ao", "cp", "gla", "glb"):
                    if n == 0 and kind != "gla":
                        pe.wait_ge({"ao": at_lo, "cp": c_lo, "glb": ys_lo}[kind], {"ao": 4 * (l + 1), "cp": l + 1, "glb": l + 1}[kind])
                    for half in range(2):
                        o = unit_bank(l, i, half)
                        for c in range(2):
                            cols = slice((2 * half + c) * P, (2 * half + c + 1) * P)
                            for k in range(4):
                                last = hi_lo(o[:, c * T:(c + 1) * T], w4[0][:, k, cols], w4[1][:, k, cols], bhi[:, k, :], blo[:, k, :], k == 0, k == 3)
                        last.then_inc(s_unit, 1)
                        if half == 0:
                            mid()
                elif kind == "fo":
                    w2 = [w[:, :].rearrange("p (k n) -> p k n", k=2) for w in (W, V)]
                    pe.wait_ge(act_lo, l * NF + n + 1)
                    if n == 0:
                        pe.wait_ge(cstd_ready, l + 1)
                    for c in range(DK):
                        o = bank[4 + c // 2][:, (c % 2) * T:(c % 2 + 1) * T]
                        for k in range(2):
                            a = (n % 2) * 2 + k
                            last = hi_lo(o, w2[0][:, k, c * P:(c + 1) * P], w2[1][:, k, c * P:(c + 1) * P], bhi[:, a, :], blo[:, a, :],
                                         n == 0 and k == 0 and c % 2 == 0, n == NF - 1 and k == 1)
                        if n == NF - 1 and c % 2 and c < DK - 1:
                            last.then_inc(ffn_sum, 1)
                        if c == 3:
                            mid()
                    last.then_inc(s_unit, 1)
                else:
                    o = unit_bank(l, i)
                    for c in range(2):
                        for k in range(DK):
                            st = [w[:, k, c * P:(c + 1) * P] for w in w8]
                            last = hi_lo(o[:, c * T:(c + 1) * T], st[0], st[1], hhi[:, k, :], hlo[:, k, :], k == 0, k == DK - 1)
                        if c == 0:
                            mid()
                    last.then_inc(s_unit, 1)

            pe.wait_ge(s_const, 32)
            for l in range(DEPTH):
                pe.wait_ge(s_rows[l], 16 * N_ROWS)
                pe.wait_ge(ldt_spread, l + 1)
                if l:
                    pe.wait_ge(vec_cp, l)
                nc.tensor.transpose(b_mod[:, 0:P], rows, ident[:, :])
                nc.tensor.transpose(b_mod[:, P:P + ST], ldtr, ident[0:ST, 0:ST])
                for c in range(CT):
                    last = nc.tensor.transpose(b_mod[:, 256 + c * 32:256 + c * 32 + TAPS], taps[:, c * P:(c + 1) * P], ident[0:TAPS, 0:TAPS])
                last.then_inc(vec_tr, 1)
                if l == 0:
                    pe.wait_ge(s_x, 32)
                    for k in range(DK):
                        for j in range(2):
                            last = nc.tensor.transpose(bank[4 + k // 2][:, (k % 2) * T + j * P:(k % 2) * T + (j + 1) * P],
                                                       h[:, 4 * j + k // 2, (k % 2) * P:(k % 2 + 1) * P], ident[:, :])
                        if k % 2:
                            last.then_inc(x_tr, 1)
            pe.wait_ge(vec_cp, DEPTH)
            mean_square(0)
            for n in range(4):
                bc_transposes(0, n)
            for k in range(DK):
                mod_block(0, 0, k)
            mod_columns(0)

            for l in range(DEPTH):
                for i in range(NB):
                    for n in mod_ends_at(l, i - 1):
                        mod_columns(n)
                    for m3 in mods_at(l, i):
                        mod_block(*m3)
                    if i == ROPE_AT:
                        rotate(l)
                    if i - 1 in ATTN_AT:
                        probs_t(l, ATTN_AT[i - 1])
                    if i in ATTN_AT:
                        scores(l, ATTN_AT[i])
                    for t in SSM_AT.get(i - 1, []):
                        ssm_out(l, t)
                    for t in SSM_AT.get(i, []):
                        ssm_in(l, t)
                    if i in (CONV_NORM_AT, CONV_NORM_AT + 1):
                        conv_stat(l, i - CONV_NORM_AT)
                    if l + 1 < DEPTH and i - 1 in BC_AT:
                        bc_transposes(l + 1, BC_AT[i - 1])
                    if NAMES[i] == ("fg", 0):
                        mean_square(2 * l + 1)

                    def mid():
                        if i - 1 in ATTN_AT:
                            attend(l, ATTN_AT[i - 1])

                    main_block(l, i, mid)
                mean_square(2 * l + 2)
            for j in range(2):
                for k in range(DK):
                    pe.wait_ge(fin_ready, k // 4 + 1)
                    last = nc.tensor.transpose(bank[4 + 2 * j + k // 4][:, (k % 4) * P:(k % 4 + 1) * P], x[:, k, j * P:(j + 1) * P], ident[:, :])
                    if k % 4 == 3:
                        last.then_inc(fin_tr, 1)

        @block.gpsimd
        def _(pool):
            for l in range(DEPTH):
                for i in range(NB):
                    if lo_engine(i) != "pool":
                        continue
                    mi = l * NB + i
                    pool.wait_ge(s_hi, mi + 1)
                    if mi >= N_LO:
                        pool.wait_ge(s_unit, used(mi - N_LO))
                    nc.gpsimd.tensor_tensor(wlo[mi % N_LO][:, :], raw[SLOT[("main", l, i)]][:, :], whi[mi % N_HI][:, :].bitcast(F32),
                                            ALU.subtract).then_inc(s_lo["pool"], 1)

        @block.scalar
        def _(act):
            step = Steps(s_act)
            fn = nc.scalar.activation

            def halves(ap):
                return ap.rearrange("p (c t) -> p c t", c=2)

            def hi(mi):
                if mi >= DEPTH * NB:
                    return
                item = ("main", *divmod(mi, NB))
                act.wait_ge(s_land[SLOT[item]], LANDED[item])
                if mi >= N_HI:
                    act.wait_ge(s_unit, used(mi - N_HI))
                fn(whi[mi % N_HI][:, :], raw[SLOT[item]][:, :], ACT.Copy).then_inc(s_hi, 1)

            def unit(l, i, n=0):
                act.wait_ge(s_unit, l * UNITS + UNIT0[i] + n + 1)
                return bank[(l * BANKS + BANK0[i] + n) % 2][:, :]

            def norm(n):
                for c in range(2):
                    if n == 0:
                        act.wait_ge(x_cp, 4)
                    elif n % 2:
                        act.wait_ge(x_mid, 4 * (n // 2) + 4)
                        act.wait_ge(hlo_ready, 2 * (3 * (n // 2) + 1) + 2)
                    else:
                        act.wait_ge(x_next, 4 * (n // 2 - 1) + 2 * c + 2)
                    fn(h[:, 4 * c:4 * c + 4, :], x[:, 4 * c:4 * c + 4, :], ACT.Square).then_inc(sq_ready, 1)
                act.wait_ge(stat_ready, n + 1)
                fn(rinv[:, :], b_y[:, 0:T], ACT.Sqrt, bias=consts[:, 7:8], scale=1.0 / D).then_inc(rms_ready, 1)

            def h_hi(n):
                for c in range(2):
                    act.wait_ge(h_ready, 2 * n + c + 1)
                    fn(hhi[:, 4 * c:4 * c + 4, :], h[:, 4 * c:4 * c + 4, :], ACT.Copy).then_inc(hhi_ready, 1)

            def mod_copy(n):
                act.wait_ge(s_modused, DK * (n + 1))
                if n:
                    act.wait_ge(mod_tr, n)
                fn(modrow[:, :], b_mod[:, :], ACT.Copy).then_inc(mod_row, 1)

            def prep(l):
                fn(small[:, 0, :], ldv[l][:, :], ACT.Exp).then_inc(prep_exp, 1)
                act.wait_ge(prep_ang, l + 1)
                fn(small[:, 3, :], small[:, 2, :], ACT.Exp).then_inc(prep_mag, 1)
                act.wait_ge(prep_arg, l + 1)
                fn(small[:, 6, :], small[:, 5, :], ACT.Sin)
                fn(small[:, 7, :], small[:, 5, :], ACT.Sin, scale=0.5).then_inc(prep_sin, 1)

            def bc_copy(l, n):
                act.wait_ge(bc_tr, 4 * l + n + 1)
                src = b_y[:, :].rearrange("p (c s) -> p c s", c=CT)
                if n < 2:
                    fn(bl[:, n], src, ACT.Copy).then_inc(bc_cp, 1)
                elif n == 2:
                    fn(cl[:, 0], src, ACT.Copy)
                    fn(cl[:, 1], src, ACT.Copy, scale=-1.0).then_inc(bc_cp, 1)
                else:
                    fn(cl[:, 2], src, ACT.Copy, scale=-1.0).then_inc(bc_cp, 1)

            def table(l, n):
                q = slice(4 * n, 4 * n + 4)
                act.wait_ge(tab_ang, 4 * l + n + 1)
                fn(stab[:, q, :], m[:, :, :], ACT.Sin, scale=2 * PI_LOW)
                fn(ctab[:, q, :], m[:, :, :], ACT.Sin, scale=PI_LOW).then_inc(tab_sin, 1)

            def softmax_exp(l, r):
                n = 4 * l + r
                act.wait_ge(mx_ready, n + 1)
                if n:
                    act.wait_ge(pt_ready, n)
                for t in range(4):
                    fn(pr[:, t, :], b_s[:, t * KEYS:(t + 1) * KEYS], ACT.Exp, bias=nmx[:, t:t + 1], scale=HEAD ** -0.5, accum_out=den[:, t:t + 1])
                fn(esink[:, :], esink[:, :], ACT.Exp).then_inc(ex_ready, 1)

            def probs_copy(l, r):
                act.wait_ge(pt_ready, 4 * l + r + 1)
                fn(pT[:, :, :], b_t[:, :].rearrange("p (t q) -> p t q", t=4), ACT.Copy).then_inc(pt_copied, 1)

            def att_hi(l, r):
                j, g = divmod(r, 2)
                p = slice(g * HEAD, (g + 1) * HEAD)
                act.wait_ge(pv_ready, 4 * l + r + 1)
                fn(bhi[p, :, j * P:(j + 1) * P], b_t[p, :].rearrange("p (t q) -> p t q", t=4), ACT.Copy).then_inc(at_hi, 1)

            def conv_mean(l):
                act.wait_ge(csum_ready, l + 1)
                fn(mean[:, :], b_t[:, 0:T], ACT.Copy, scale=1.0 / CW).then_inc(mean_ready, 1)
                act.wait_ge(cent_ready, l + 1)
                fn(uc[:, :, 0:T], yc[:, :, :], ACT.Square).then_inc(csq_ready, 1)

            def conv_silu(l):
                act.wait_ge(cvar_ready, l + 1)
                fn(mean[:, :], b_t[:, T:2 * T], ACT.Sqrt, bias=consts[:, 7:8], scale=1.0 / CW).then_inc(cstd_ready, 1)
                act.wait_ge(cnorm_ready, l + 1)
                for c in range(CT):
                    last = fn(yc[:, c, :], yc[:, c, :], ACT.Silu, scale=vec[l][:, R_LNG + c:R_LNG + c + 1], bias=vec[l][:, R_LNB + c:R_LNB + c + 1])
                last.then_inc(csilu_ready, 1)
                act.wait_ge(csilu_ready, l + 1)
                act.wait_ge(s_unit, used(l * NB + AT[("ao", 1)]))
                fn(bhi[:, :, :], yc[:, :, :], ACT.Copy).then_inc(c_hi, 1)

            def ssm_hi(l):
                act.wait_ge(y_used, 2 * (l + 1))
                act.wait_ge(s_unit, used(l * NB + AT[("cp", 1)]))
                fn(bhi[:, :, :], ys[:, :, :], ACT.Copy).then_inc(ys_hi, 1)

            def post(l, i):
                kind, n = NAMES[i]
                two = slice(2 * n, 2 * n + 2)
                if kind == "su":
                    fn(u_ssm[:, two, :], halves(unit(l, i)), ACT.Copy).then_inc(u_ready, 1)
                elif kind == "q":
                    fn(qT[:, two, :], halves(unit(l, i)), ACT.Copy).then_inc(qk_ready, 1)
                elif kind == "kv":
                    fn(kT[:, :], unit(l, i)[:, 0:T], ACT.Copy).then_inc(qk_ready, 1)
                elif kind == "cb":
                    if 2 * l + n:
                        act.wait_ge(uc_ready, 2 * l + n)
                    fn(tmp[:, :, :], halves(unit(l, i)), ACT.Sigmoid).then_inc(sigb_ready, 1)
                elif kind in ("ga", "gc", "gs"):
                    b = unit(l, i)
                    if kind != "ga":
                        act.wait_ge(ao_read if kind == "gc" else cp_read, 4 * l + n + 1)
                    fn(gate[:, two, :], halves(b), ACT.Sigmoid).then_inc(gate_ready, 1)
                elif kind == "glb":
                    for half in range(2):
                        b = unit(l, i, half)
                        if n:
                            act.wait_ge(gl_read, 4 * l + half + 1)
                        fn(prod[half][:, 0:2, :], halves(b), ACT.Sigmoid).then_inc(glsig_ready, 1)
                elif kind == "fg":
                    b = unit(l, i)
                    if n >= 2:
                        act.wait_ge(act_lo, l * NF + n - 1)
                    a = 2 * (n % 2)
                    fn(gate[:, a:a + 2, :], halves(b), ACT.Silu).then_inc(silu_ready, 1)
                elif kind == "fu":
                    act.wait_ge(act_ready, l * NF + n + 1)
                    if n >= 2:
                        act.wait_ge(s_unit, used(l * NB + AT[("fo", n - 2)]))
                    a = 2 * (n % 2)
                    fn(bhi[:, a:a + 2, :], gate[:, a:a + 2, :], ACT.Copy).then_inc(act_hi, 1)

            act.wait_ge(vec_cp, 1)
            fn(cact[:, :], vec[0][:, R_C:R_C + DK], ACT.Silu).then_inc(silu_c, 1)
            for n in range(4):
                act.wait_ge(x_tr, n + 1)
                fn(x[:, 2 * n:2 * n + 2, :], halves(bank[4 + n][:, :]), ACT.Copy).then_inc(x_cp, 1)
            act.wait_ge(s_const2, 16 * 5)
            norm(0)
            prep(0)
            for n in range(4):
                bc_copy(0, n)
            act.wait_ge(rope_ang, 1)
            fn(sinr[:, :], tmp[:, 0, :], ACT.Sin)
            fn(cosr[:, :], tmp[:, 0, :], ACT.Sin, scale=0.5).then_inc(rope_sin, 1)
            for n in range(4):
                table(0, n)
            mod_copy(0)
            for mi in range(AHEAD):
                hi(mi)
            h_hi(0)
            for l in range(DEPTH):
                for i in range(NB):
                    hi(l * NB + i + AHEAD)
                    for n in mod_ends_at(l, i):
                        mod_copy(n)
                    if i - 1 in ATTN_AT:
                        probs_copy(l, ATTN_AT[i - 1])
                    if i in ATTN_AT:
                        softmax_exp(l, ATTN_AT[i])
                    if i - 1 in ATTN_AT:
                        att_hi(l, ATTN_AT[i - 1])
                    if i == CONV_NORM_AT:
                        conv_mean(l)
                    if i == CONV_NORM_AT + 1:
                        conv_silu(l)
                    if i == AT[("gs", 3)]:
                        ssm_hi(l)
                    if l + 1 < DEPTH:
                        if i == PREP_AT:
                            prep(l + 1)
                        if i - 1 in BC_AT:
                            bc_copy(l + 1, BC_AT[i - 1])
                        if i in TABLE_AT:
                            table(l + 1, TABLE_AT[i])
                    post(l, i)
                    if NAMES[i] == ("gla", 1):
                        h_hi(3 * l + 1)
                    if NAMES[i] == ("wo", 3):
                        norm(2 * l + 1)
                        h_hi(3 * l + 2)
                norm(2 * l + 2)
                if l + 1 < DEPTH:
                    h_hi(3 * l + 3)
            for n in range(4):
                act.wait_ge(fin_tr, n + 1)
                if n == 0:
                    act.wait_ge(stat_ready, 2 * DEPTH + 1)
                fn(h[:, 2 * n:2 * n + 2, :], halves(bank[4 + n][:, :]), ACT.Copy).then_inc(fin_cp, 1)

        @block.vector
        def _(dve):
            step = Steps(s_dve)
            V = nc.vector

            def then(ins):
                dve.wait_ge(s_dve, step(ins))

            def bcast(ap, n):
                return ap.rearrange("p (a o) -> p a o", o=1).to_broadcast([ap.shape[0], ap.shape[1], n])

            def rows4(ap, n):
                return ap.rearrange("p (o t) -> p o t", o=1).to_broadcast([P, n, T])

            def halves(ap):
                return ap.rearrange("p (c t) -> p c t", c=2)

            def lo(mi):
                if mi >= DEPTH * NB or lo_engine(mi % NB) != "dve":
                    return
                dve.wait_ge(s_hi, mi + 1)
                if mi >= N_LO:
                    dve.wait_ge(s_unit, used(mi - N_LO))
                V.tensor_tensor(wlo[mi % N_LO][:, :], raw[SLOT[("main", *divmod(mi, NB))]][:, :], whi[mi % N_HI][:, :].bitcast(F32),
                                ALU.subtract).then_inc(s_lo["dve"], 1)

            def unit(l, i, n=0):
                dve.wait_ge(s_unit, l * UNITS + UNIT0[i] + n + 1)
                return bank[(l * BANKS + BANK0[i] + n) % 2][:, :]

            def reduce_angle(dst, src, k):
                then(V.tensor_scalar(k, src, 1.0 / TWO_PI, ROUND, ALU.mult, ALU.add))
                then(V.tensor_scalar(k, k, ROUND, None, ALU.subtract))
                then(V.scalar_tensor_tensor(out=dst, in0=k, scalar=-C1, in1=src, op0=ALU.mult, op1=ALU.add))
                then(V.scalar_tensor_tensor(out=dst, in0=k, scalar=-C2, in1=dst, op0=ALU.mult, op1=ALU.add))
                then(V.scalar_tensor_tensor(out=dst, in0=k, scalar=-C3, in1=dst, op0=ALU.mult, op1=ALU.add))
                return V.tensor_scalar(dst, dst, PI_LOW, -PI_LOW, ALU.min, ALU.max)

            def prep(l):
                a_re, a_im = vec[l][:, R_ARE:R_ARE + ST], vec[l][:, R_AIM:R_AIM + ST]
                S = [small[:, n, :] for n in range(20)]
                dt, th, dr, mag, k, ang, sn, sh, cs, turns = S[:10]
                nre, nim, d1, d2, fre, fim, t1, t2 = S[10:18]
                tt = V.tensor_tensor
                dve.wait_ge(prep_exp, l + 1)
                tt(dr, dt, a_re, ALU.mult).then_inc(prep_ang, 1)
                then(tt(th, dt, a_im, ALU.mult))
                reduce_angle(ang, th, k).then_inc(prep_arg, 1)
                dve.wait_ge(prep_arg, l + 1)
                then(V.tensor_scalar(turns, ang, 1.0 / TWO_PI, None, ALU.mult))
                then(tt(d1, a_re, a_re, ALU.mult))
                then(tt(d2, a_im, a_im, ALU.mult))
                then(tt(d1, d1, d2, ALU.add))
                then(V.reciprocal(d2, d1))
                dve.wait_ge(prep_mag, l + 1)
                dve.wait_ge(prep_sin, l + 1)
                then(tt(cs, sh, sh, ALU.mult))
                then(V.tensor_scalar(cs, cs, -2.0, 1.0, ALU.mult, ALU.add))
                then(tt(nre, mag, cs, ALU.mult))
                then(V.tensor_scalar(nre, nre, 1.0, None, ALU.subtract))
                then(tt(nim, mag, sn, ALU.mult))
                then(tt(t1, nre, a_re, ALU.mult))
                then(tt(t2, nim, a_im, ALU.mult))
                then(tt(t1, t1, t2, ALU.add))
                then(tt(fre, t1, d2, ALU.mult))
                then(tt(t1, nim, a_re, ALU.mult))
                then(tt(t2, nre, a_im, ALU.mult))
                then(tt(t1, t1, t2, ALU.subtract))
                then(tt(fim, t1, d2, ALU.mult))

            def bc_source(l, n):
                fre, fim = small[:, 14, :], small[:, 15, :]
                tt = V.tensor_tensor
                dve.wait_ge(s_bc, 64 * (l + 1))
                if n < 2:
                    if n == 0:
                        then(V.memset(bsrc, 0.0))
                    else:
                        dve.wait_ge(bc_src, 4 * l + 1)
                    a, b, op = (0, 1, ALU.subtract) if n == 0 else (1, 0, ALU.add)
                    then(tt(bt[:, 0], bn[:, a], bcast(fre, GROUP), ALU.mult))
                    then(tt(bt[:, 1], bn[:, b], bcast(fim, GROUP), ALU.mult))
                    if n:
                        dve.wait_ge(bc_tr, 4 * l + 1)
                    for g in range(2):
                        p = slice(g * HEAD, (g + 1) * HEAD)
                        last = tt(bsrc[p, :, g * GROUP:(g + 1) * GROUP], bt[p, 0], bt[p, 1], op)
                else:
                    if n == 3:
                        dve.wait_ge(bc_src, 4 * l + 3)
                        dve.wait_ge(bc_tr, 4 * l + 3)
                    for g in range(2):
                        last = V.tensor_scalar(csrc[:, :, g * HEAD:(g + 1) * HEAD], cn[:, n - 2], consts[:, 4 + g:5 + g], None, ALU.mult)
                last.then_inc(bc_src, 1)

            def table(l, n):
                k = prod[0][:, :, :]
                if l or n:
                    dve.wait_ge(tab_sin, 4 * l + n)
                then(V.tensor_tensor(m[:, :, :], rows4(iota[:, :], 4), bcast(small[:, 9, 4 * n:4 * n + 4], T), ALU.mult))
                then(V.tensor_scalar(k, m[:, :, :], ROUND, None, ALU.add))
                then(V.tensor_scalar(k, k, ROUND, None, ALU.subtract))
                V.tensor_tensor(m[:, :, :], m[:, :, :], k, ALU.subtract).then_inc(tab_ang, 1)

            def table_cos(l, n):
                q = slice(4 * n, 4 * n + 4)
                dve.wait_ge(tab_sin, 4 * l + n + 1)
                then(V.tensor_tensor(ctab[:, q, :], ctab[:, q, :], ctab[:, q, :], ALU.mult))
                then(V.tensor_scalar(ctab[:, q, :], ctab[:, q, :], -2.0, 1.0, ALU.mult, ALU.add))

            def mod_vectors(l, ng):
                n = 3 * l + ng
                dve.wait_ge(mod_tr, n + 1)
                c0 = 16 * ng
                V.tensor_tensor(modv[:, c0:c0 + 16].rearrange("p (q j) -> p j q", q=4), b_mod[:, 0:16].rearrange("p (j q) -> p j q", q=4),
                                vec[l][:, c0:c0 + 16].rearrange("p (q j) -> p j q", q=4), ALU.add).then_inc(mod_ready, 1)
                dve.wait_ge(mod_ready, n + 1)
                if ng != 1:
                    s, m0, r0 = (scale1, M_SC1, R_N1) if ng == 0 else (scale2, M_SC2, R_N2)
                    then(V.scalar_tensor_tensor(out=s[:, :], in0=modv[:, m0:m0 + DK], scalar=1.0, in1=vec[l][:, r0:r0 + DK], op0=ALU.add, op1=ALU.mult))

            def norm(n, s, shift):
                dve.wait_ge(rms_ready, n + 1)
                then(V.reciprocal(rinv[:, :], rinv[:, :]))
                for c in range(2):
                    step(V.tensor_tensor(h[:, 4 * c:4 * c + 4, :], x[:, 4 * c:4 * c + 4, :], rows4(rinv[:, :], 4), ALU.mult))
                for c in range(2):
                    dve.wait_ge(s_dve, step.n - 1 + c)
                    for k in range(4 * c, 4 * c + 4):
                        last = V.tensor_scalar(h[:, k, :], h[:, k, :], s[:, k:k + 1], modv[:, shift + k:shift + k + 1], ALU.mult, ALU.add)
                    last.then_inc(h_ready, 1)

            def h_lo(n):
                for c in range(2):
                    dve.wait_ge(hhi_ready, 2 * n + c + 1)
                    q = slice(4 * c, 4 * c + 4)
                    V.tensor_tensor(hlo[:, q, :], h[:, q, :], hhi[:, q, :].bitcast(F32), ALU.subtract).then_inc(hlo_ready, 1)

            def rope(l):
                for c in range(3):
                    dve.wait_ge(rot_ready, 3 * l + c + 1)
                    w = 2 if c < 2 else 1
                    src = halves((b_s, b_t, b_s)[c][:, :])[:, 0:w, :]
                    q = qT[:, 2 * c:2 * c + 2, :] if c < 2 else kT[:, :].rearrange("p (o t) -> p o t", o=1)
                    step(V.tensor_tensor(rtmp[:, 0:w, :], src, rows4(sinr[:, :], w), ALU.mult))
                    then(V.tensor_tensor(q, q, rows4(cosr[:, :], w), ALU.mult))
                    V.tensor_tensor(q, q, rtmp[:, 0:w, :], ALU.add).then_inc(rope_ready, 1)
                    dve.wait_ge(rope_ready, 3 * l + c + 1)

            def softmax_max(l, r):
                n = 4 * l + r
                j, g = divmod(r, 2)
                sk = sink[:, l, 4 * g:4 * g + 4]
                b = b_s[:, :].rearrange("p (t k) -> p t k", t=4)
                dve.wait_ge(sc_ready, n + 1)
                if j == 0:
                    then(V.memset(b[0:CHUNK, :, CHUNK:KEYS], NEG))
                then(V.tensor_reduce(mx[:, :], b, AX_X, ALU.max))
                then(V.scalar_tensor_tensor(out=mx[:, :], in0=mx[:, :], scalar=HEAD ** -0.5, in1=sk, op0=ALU.mult, op1=ALU.max))
                step(V.tensor_tensor(esink[:, :], sk, mx[:, :], ALU.subtract))
                V.tensor_scalar(nmx[:, :], mx[:, :], -1.0, None, ALU.mult).then_inc(mx_ready, 1)

            def softmax_norm(l, r):
                dve.wait_ge(ex_ready, 4 * l + r + 1)
                then(V.tensor_tensor(den[:, :], den[:, :], esink[:, :], ALU.add))
                then(V.reciprocal(rden[:, :], den[:, :]))
                V.tensor_tensor(pr[:, :, :], pr[:, :, :], bcast(rden[:, :], KEYS), ALU.mult).then_inc(pr_ready, 1)

            def att_lo(l, r):
                j, g = divmod(r, 2)
                p = slice(g * HEAD, (g + 1) * HEAD)
                dve.wait_ge(at_hi, 4 * l + r + 1)
                V.tensor_tensor(blo[p, :, j * P:(j + 1) * P], b_t[p, :].rearrange("p (t q) -> p t q", t=4),
                                bhi[p, :, j * P:(j + 1) * P].bitcast(F32), ALU.subtract).then_inc(at_lo, 1)

            def ssm(l, t):
                n = l * ST + t
                cs, sn = rows4(ctab[:, t, :], 2), rows4(stab[:, t, :], 2)
                r = small[:, 3, t:t + 1].to_broadcast([P, T])
                pd = prod[t % 2]
                dve.wait_ge(bu_ready, n + 1)
                bu = halves(b_bu[t % 2][:, :])
                step(V.tensor_tensor(m[:, 0:2, :], bu, cs, ALU.mult))
                V.tensor_tensor(m[:, 2:4, :], bu, sn, ALU.mult).then_inc(bu_used, 1)
                dve.wait_ge(bu_used, n + 1)
                step(V.tensor_tensor(m[:, 0, :], m[:, 0, :], m[:, 3, :], ALU.add))
                step(V.tensor_tensor(m[:, 1, :], m[:, 1, :], m[:, 2, :], ALU.subtract))
                dve.wait_ge(s_dve, step.n - 1)
                step(V.tensor_tensor_scan(m[:, 0, :], r, m[:, 0, :], 0.0, ALU.mult, ALU.add))
                dve.wait_ge(s_dve, step.n - 1)
                then(V.tensor_tensor_scan(m[:, 1, :], r, m[:, 1, :], 0.0, ALU.mult, ALU.add))
                if n >= 2:
                    dve.wait_ge(y_ready, n - 1)
                V.tensor_tensor(pd[:, 0:2, :], m[:, 0:2, :], cs, ALU.mult)
                V.tensor_tensor(pd[:, 2:4, :], m[:, 0:2, :], sn, ALU.mult).then_inc(prod_ready, 1)
                dve.wait_ge(prod_ready, n + 1)

            def ssm_y(l, half):
                n = 2 * l + half
                dve.wait_ge(y_ready, 8 * (n + 1))
                for c in range(2):
                    k = 2 * half + c
                    last = V.scalar_tensor_tensor(out=ys[:, k, :], in0=u_ssm[:, k, :], scalar=vec[l][:, R_D + k:R_D + k + 1],
                                                  in1=b_y[:, c * T:(c + 1) * T], op0=ALU.mult, op1=ALU.add)
                last.then_inc(y_used, 1)

            def conv(l, pair, seg):
                for k in range(8 * seg, min(8 * seg + 8, TAPS)):
                    for c in (2 * pair, 2 * pair + 1):
                        w = tapv[l][:, c, k:k + 1]
                        if k == 0:
                            last = V.tensor_scalar(yc[:, c, :], uc[:, c, 0:T], w, vec[l][:, R_DWB + c:R_DWB + c + 1], ALU.mult, ALU.add)
                        else:
                            dve.wait_ge(s_dve, step.n - 1)
                            last = V.scalar_tensor_tensor(out=yc[:, c, :], in0=uc[:, c, k:k + T], scalar=w, in1=yc[:, c, :], op0=ALU.mult, op1=ALU.add)
                        if (k, c) == (TAPS - 1, CT - 1):
                            last.then_inc(conv_ready, 1)
                        else:
                            step(last)

            def conv_center(l):
                dve.wait_ge(mean_ready, l + 1)
                V.tensor_tensor(yc[:, :, :], yc[:, :, :], rows4(mean[:, :], 4), ALU.subtract).then_inc(cent_ready, 1)

            def conv_norm(l):
                dve.wait_ge(cstd_ready, l + 1)
                then(V.reciprocal(mean[:, :], mean[:, :]))
                V.tensor_tensor(yc[:, :, :], yc[:, :, :], rows4(mean[:, :], 4), ALU.mult).then_inc(cnorm_ready, 1)
                dve.wait_ge(c_hi, l + 1)
                V.tensor_tensor(blo[:, :, :], yc[:, :, :], bhi[:, :, :].bitcast(F32), ALU.subtract).then_inc(c_lo, 1)

            def ssm_lo(l):
                dve.wait_ge(ys_hi, l + 1)
                V.tensor_tensor(blo[:, :, :], ys[:, :, :], bhi[:, :, :].bitcast(F32), ALU.subtract).then_inc(ys_lo, 1)

            def post(l, i):
                kind, n = NAMES[i]
                if kind == "kv":
                    V.tensor_copy(vv[:, :, :], unit(l, i, 1)[:, 0:3 * P].rearrange("p (c d) -> p c d", c=3)).then_inc(v_ready, 1)
                elif kind == "ca":
                    b = unit(l, i)
                    dve.wait_ge(sigb_ready, 2 * l + n + 1)
                    V.tensor_tensor(uc[:, 2 * n:2 * n + 2, PAD:PAD + T], halves(b), tmp[:, :, :], ALU.mult).then_inc(uc_ready, 1)
                    dve.wait_ge(uc_ready, 2 * l + n + 1)
                elif kind in ("ao", "cp", "gla"):
                    for half in range(2):
                        c = 2 * (2 * n + half)
                        q = slice(c, c + 2)
                        v = 4 * l + 2 * n + half + 1
                        b = halves(unit(l, i, half))
                        if half == 0 and n == 0:
                            dve.wait_ge(gate_ready, 12 * l + {"ao": 4, "cp": 8, "gla": 12}[kind])
                        if kind == "ao":
                            V.tensor_tensor(h[:, q, :], b, gate[:, q, :], ALU.mult).then_inc(ao_read, 1)
                        elif kind == "cp":
                            V.tensor_tensor(tmp[:, :, :], b, gate[:, q, :], ALU.mult).then_inc(cp_read, 1)
                            dve.wait_ge(cp_read, v)
                            then(V.tensor_tensor(h[:, q, :], h[:, q, :], tmp[:, :, :], ALU.add))
                        else:
                            dve.wait_ge(glsig_ready, v)
                            V.tensor_tensor(tmp[:, :, :], b, prod[half][:, 0:2, :], ALU.mult).then_inc(gl_read, 1)
                            dve.wait_ge(gl_read, v)
                            then(V.tensor_tensor(tmp[:, :, :], tmp[:, :, :], gate[:, q, :], ALU.mult))
                            last = V.tensor_tensor(h[:, q, :], h[:, q, :], tmp[:, :, :], ALU.add)
                            if half:
                                last.then_inc(h_ready, 1)
                                dve.wait_ge(h_ready, 2 * (3 * l + 1) + n + 1)
                            else:
                                then(last)
                elif kind == "wo":
                    b = unit(l, i)
                    for c in range(2):
                        k = 2 * n + c
                        last = V.scalar_tensor_tensor(out=x[:, k, :], in0=b[:, c * T:(c + 1) * T], scalar=modv[:, M_G1 + k:M_G1 + k + 1],
                                                      in1=x[:, k, :], op0=ALU.mult, op1=ALU.add)
                    last.then_inc(x_mid, 1)
                elif kind == "fu":
                    b = unit(l, i)
                    a = slice(2 * (n % 2), 2 * (n % 2) + 2)
                    v = l * NF + n + 1
                    dve.wait_ge(silu_ready, v)
                    V.tensor_tensor(gate[:, a, :], halves(b), gate[:, a, :], ALU.mult).then_inc(act_ready, 1)
                    dve.wait_ge(act_hi, v)
                    V.tensor_tensor(blo[:, a, :], gate[:, a, :], bhi[:, a, :].bitcast(F32), ALU.subtract).then_inc(act_lo, 1)
                elif kind == "fo" and n == NF - 1:
                    for k in range(DK):
                        if k % 2 == 0:
                            if k < DK - 2:
                                dve.wait_ge(ffn_sum, 3 * l + k // 2 + 1)
                            else:
                                dve.wait_ge(s_unit, used(l * NB + i))
                        last = V.scalar_tensor_tensor(out=x[:, k, :], in0=bank[4 + k // 2][:, (k % 2) * T:(k % 2 + 1) * T],
                                                      scalar=modv[:, M_G2 + k:M_G2 + k + 1], in1=x[:, k, :], op0=ALU.mult, op1=ALU.add)
                        if k % 2:
                            last.then_inc(x_next, 1)

            for l in range(DEPTH):
                dve.wait_ge(s_rows[l], 16 * N_ROWS)
                V.tensor_copy(ldtr.rearrange("s (g n) -> s g n", g=2), bcast(ldt[:, :], HEAD)).then_inc(ldt_spread, 1)
                dve.wait_ge(vec_tr, l + 1)
                V.tensor_copy(vec[l][:, :], b_mod[:, 0:P])
                V.tensor_copy(ldv[l][:, :], b_mod[:, P:P + ST])
                V.tensor_copy(tapv[l][:, :, :], b_mod[:, 256:384].rearrange("p (c k) -> p c k", c=CT)[:, :, 0:TAPS]).then_inc(vec_cp, 1)
                if l == 0:
                    dve.wait_ge(silu_c, 1)
                    V.tensor_copy(cact32[:, :, :], bcast(cact[:, :], 32)).then_inc(c_ready, 1)
            prep(0)
            for n in range(4):
                bc_source(0, n)
            dve.wait_ge(s_const2, 16 * 5)
            then(V.tensor_copy(tmp[:, 1, :], posi))
            then(V.tensor_scalar(tmp[:, 1, :], tmp[:, 1, :], consts[:, 6:7], None, ALU.mult))
            reduce_angle(tmp[:, 0, :], tmp[:, 1, :], rtmp[:, 0, :]).then_inc(rope_ang, 1)
            dve.wait_ge(rope_sin, 1)
            then(V.tensor_tensor(cosr[:, :], cosr[:, :], cosr[:, :], ALU.mult))
            then(V.tensor_scalar(cosr[:, :], cosr[:, :], -2.0, 1.0, ALU.mult, ALU.add))
            for n in range(4):
                table(0, n)
                table_cos(0, n)
            mod_vectors(0, 0)
            norm(0, scale1, M_SH1)
            h_lo(0)
            for l in range(DEPTH):
                for i in range(NB):
                    lo(l * NB + i + AHEAD)
                    for n in mod_ends_at(l, i - 1):
                        mod_vectors(*divmod(n, 3))
                    if i == AT[("cb", 0)]:
                        then(V.memset(uc[:, :, 0:PAD], 0.0))
                    if i == ROPE_AT:
                        rope(l)
                    if i in ATTN_AT:
                        softmax_max(l, ATTN_AT[i])
                    for t in SSM_AT.get(i - 1, []):
                        if t % 8 == 7:
                            ssm_y(l, t // 8)
                    if i - 1 in ATTN_AT:
                        att_lo(l, ATTN_AT[i - 1])
                    for t in SSM_AT.get(i, []):
                        ssm(l, t)
                    if i in ATTN_AT:
                        softmax_norm(l, ATTN_AT[i])
                    if i in CONV_AT:
                        conv(l, *CONV_AT[i])
                    if i == CONV_NORM_AT:
                        conv_center(l)
                    if i == CONV_NORM_AT + 1:
                        conv_norm(l)
                    if i == AT[("gs", 3)]:
                        ssm_lo(l)
                    if l + 1 < DEPTH:
                        if i == PREP_AT:
                            prep(l + 1)
                        if i in BC_AT:
                            bc_source(l + 1, BC_AT[i])
                        if i in TABLE_AT:
                            table(l + 1, TABLE_AT[i])
                            table_cos(l + 1, TABLE_AT[i])
                    post(l, i)
                    if NAMES[i] == ("gla", 1):
                        h_lo(3 * l + 1)
                    if i + 1 < NB and NAMES[i] == ("wo", 3):
                        norm(2 * l + 1, scale2, M_SH2)
                        h_lo(3 * l + 2)
                if l + 1 < DEPTH:
                    norm(2 * l + 2, scale1, M_SH1)
                    h_lo(3 * l + 3)
            dve.wait_ge(rms_ready, 2 * DEPTH + 1)
            then(V.reciprocal(rinv[:, :], rinv[:, :]))
            for c in range(2):
                step(V.tensor_tensor(x[:, 4 * c:4 * c + 4, :], x[:, 4 * c:4 * c + 4, :], rows4(rinv[:, :], 4), ALU.mult))
            for c in range(2):
                dve.wait_ge(s_dve, step.n - 1 + c)
                for k in range(4 * c, 4 * c + 4):
                    last = V.tensor_scalar(x[:, k, :], x[:, k, :], vec[0][:, R_FIN + k:R_FIN + k + 1], None, ALU.mult)
                last.then_inc(fin_ready, 1)


_INS = ("x", "c", "positions", "w_mod", "b_mod", "norm1_g", "w_in", "attn_sinks", "w_attn_o", "conv_dw_w", "conv_dw_b",
        "conv_ln_g", "conv_ln_b", "conv_pw_w", "ssm_a_re", "ssm_a_im", "ssm_log_dt", "ssm_b_re", "ssm_b_im", "ssm_c_re",
        "ssm_c_im", "ssm_d", "ssm_glu_a", "ssm_glu_b", "w_out", "norm2_g", "w_ffn_in", "w_ffn_out", "final_norm_g")


def constants():
    p = np.arange(P)
    small = np.zeros((P, 16), np.float32)
    small[32 * np.arange(4), np.arange(4)] = 1.0
    small[:, 4] = (p // GROUP) % 2 == 0
    small[:, 5] = (p // GROUP) % 2 == 1
    half = ROPE_DIM // 2
    inv = np.float32(THETA) ** (-np.arange(0, ROPE_DIM, 2, dtype=np.float32) / np.float32(ROPE_DIM))
    small[:, 6] = np.where(p % HEAD < ROPE_DIM, inv[p % half], 0.0)
    small[:, 7] = EPS
    rot = np.zeros((P, P), np.float32)
    for g in range(NKV):
        for j in range(half):
            rot[g * HEAD + half + j, g * HEAD + j] = -1.0
            rot[g * HEAD + j, g * HEAD + half + j] = 1.0
    iota = np.broadcast_to(np.arange(T, dtype=np.float32), (P, T))
    return {"c_ident": np.eye(P, dtype=np.float32), "c_small": small, "c_ones": np.ones((P, P), np.float32), "c_rot": rot,
            "c_iota": np.ascontiguousarray(iota)}


def kernel(**inputs):
    import concourse.bacc as _bacc
    from concourse.bass_utils import run_bass_kernel_spmd as _run

    nc = _bacc.Bacc("TRN2", target_bir_lowering=False, num_devices=1)
    arrays = {name: np.ascontiguousarray(inputs[name]) for name in _INS} | constants()
    A = {n: nc.dram_tensor(f"in_{n}", a.shape, mybir.dt.from_np(a.dtype), kind="ExternalInput").ap() for n, a in arrays.items()}
    out = nc.dram_tensor("out_0", (1, T, D), F32, kind="ExternalOutput").ap()
    trunk(nc, A, out)
    r = _run(nc, [{f"in_{n}": a for n, a in arrays.items()}], core_ids=[0])
    return r.results[0]["out_0"]
```

```python
from contextlib import ExitStack

import numpy as np
import concourse.bass as bass
from concourse import mybir

ALU = mybir.AluOpType
ACT = mybir.ActivationFunctionType
F32 = mybir.dt.float32
F32R = mybir.dt.float32r
I32 = mybir.dt.int32
AX_X = mybir.AxisListType.X

P = 128
D = 1024
T = 256
DEPTH = 2
DK = D // P
HEAD = 64
NQ = 8
NKV = 2
CHUNK = 64
KEYS = 128
TAPS = 31
PAD = TAPS - 1
CW = 512
CT = CW // P
ST = 16
GROUP = 16
DFF = 2816
FK = DFF // P
EPS = 1e-6
NEG = -1e30
ROPE_DIM = 16
THETA = 500000.0
OFF_K, OFF_V, OFF_CA, OFF_CB, OFF_SU, OFF_G = 512, 640, 768, 1280, 1792, 2304
BC = 256
MODC = 2048

ROUND = 12582912.0
TWO_PI = 6.283185307179586
PI_LOW = float(np.nextafter(np.float32(np.pi), np.float32(0)))
C1 = 6.28125
C2 = float(np.float32(np.round((TWO_PI - C1) * 2**22) / 2**22))
C3 = float(np.float32(TWO_PI - C1 - C2))

R_BMOD, R_N1, R_N2, R_DWB, R_LNG, R_LNB, R_D, R_ARE, R_AIM, R_FIN, R_C = 0, 48, 56, 64, 68, 72, 76, 80, 96, 112, 120
M_SH1, M_SC1, M_G1, M_SH2, M_SC2, M_G2 = 0, 8, 16, 24, 32, 40


def block_names():
    names = [("su", 0), ("q", 0), ("q", 1), ("kv", 0), ("cb", 0), ("ca", 0), ("cb", 1), ("ca", 1)]
    names += [("ga", n) for n in range(4)] + [("su", 1), ("ao", 0), ("ao", 1)]
    names += [("gc", n) for n in range(4)] + [("cp", 0), ("cp", 1)]
    names += [("gs", n) for n in range(4)] + [("glb", 0), ("gla", 0), ("glb", 1), ("gla", 1)]
    names += [("wo", n) for n in range(4)]
    for n in range(FK // 2):
        names += [("fg", n), ("fu", n)]
        if n:
            names += [("fo", n - 1)]
    return names + [("fo", FK // 2 - 1)]


NAMES = block_names()
NB = len(NAMES)
AT = {name: i for i, name in enumerate(NAMES)}
N_UNITS = {"ao": 2, "cp": 2, "gla": 2, "glb": 2}
UNIT0 = [sum(N_UNITS.get(NAMES[j][0], 1) for j in range(i)) for i in range(NB + 1)]
BANK0 = [sum(N_UNITS.get(NAMES[j][0], 1) for j in range(i) if NAMES[j][0] != "fo") for i in range(NB + 1)]
UNITS, BANKS = UNIT0[NB], BANK0[NB]
NF = FK // 2

H_PER_LAYER, H0 = 2 * DK + 4, {"su": 0, "wo": DK, "fg": DK + 4}

SSM_PAIRS = [3, 7, 11, 15, 34, 38, 42, 45]
SSM_IN_AT = {t: n for n, t in enumerate(SSM_PAIRS)}
SSM_OUT_AT = {t + 4: n for n, t in enumerate(SSM_PAIRS)}
SSM_AT = {t + 2 * c: 2 * n + c for n, t in enumerate(SSM_PAIRS) for c in range(2)}
SSM_Y_AT = {SSM_PAIRS[4 * n + 3] + 4: n for n in range(2)}
SSM_SPLIT_AT = SSM_PAIRS[7] + 4
ROPE_Q_AT, ROPE_K_AT = 8, 9
PROBS_LAG = 2
SCORES_AT = {11 + 4 * r: r for r in range(4)}
PROBS_AT = {t + PROBS_LAG: r for t, r in SCORES_AT.items()}
ATTEND_AT = {t + PROBS_LAG + 1: r for t, r in SCORES_AT.items()}
CONV_AT = {18 + n: divmod(n, 8) for n in range(16)}
CONV_MEAN_AT, CONV_VAR_AT = 35, 36
MOD_AT = {0: {5 + 3 * (n // 2) + n % 2: (1, n) for n in range(DK)} | {18 + 3 * (n // 2) + n % 2: (2, n) for n in range(DK)},
          1: {6 + 3 * n: (2, n) for n in range(DK)}}
BEFORE_NORM = (AT[("wo", 3)], NB - 1)
MEAN_SQUARE_AT = {2 * AT[("wo", 2)] + 1 + c: c for c in range(3)}
PREP_AT = AT[("fg", 1)]
NORM_MODS = 2
NEXT_THIRDS = [(ng, k) for ng in range(2) for k in range(DK)]
NEXT_MOD_AT = {PREP_AT + 2 + 2 * n + 2 * (n >= DK - NORM_MODS): NEXT_THIRDS[NORM_MODS + n] for n in range(2 * DK - 2 * NORM_MODS)}
BC_AT = {PREP_AT + 2 + 3 * n: n for n in range(4)}
BC_TR_AT = {i + 2: n for i, n in BC_AT.items()}
TABLE_AT = {PREP_AT + 14 + 4 * n: n for n in range(4)}
FIRST_TABLE_AT = {0: 0, 2: 1, 5: 2, 6: 3}

N_LOADS = {"q": 4, "ao": 2}
N_RAW, N_HI, N_LO = 4, 3, 2
AHEAD = 2


def lo_engine(i):
    return "pool" if i < PREP_AT + 1 else "dve"


def mods_at(l, i):
    found = [(l, *MOD_AT[min(l, 1)][i])] if i in MOD_AT[min(l, 1)] else []
    if l and i == 0:
        found = [(l, *m) for m in NEXT_THIRDS[-NORM_MODS:]]
    if l + 1 < DEPTH:
        if NAMES[i] == ("fg", 0):
            found = [(l + 1, *m) for m in NEXT_THIRDS[:NORM_MODS]]
        elif i in NEXT_MOD_AT:
            found.append((l + 1, *NEXT_MOD_AT[i]))
    return found


def mod_ends_at(l, i):
    return [3 * m[0] + m[1] for m in mods_at(l, i) if m[2] == DK - 1] if i >= 0 else []


def used(mi):
    return (mi // NB) * UNITS + UNIT0[mi % NB + 1]


def plan_loads():
    items = [("mod", 0, 0, k) for k in range(N_RAW)]
    for l in range(DEPTH):
        for i in range(NB):
            items += [("mod", *m) for m in mods_at(l, i)]
            items.append(("main", l, i))
    count, slot_of, landed, after = [0] * N_RAW, {}, {}, {}
    owner = [None] * N_RAW
    for n, item in enumerate(items):
        s = n % N_RAW
        count[s] += 16 * (N_LOADS.get(NAMES[item[2]][0], 1) if item[0] == "main" else 1)
        slot_of[item], landed[item], after[item] = s, count[s], owner[s]
        owner[s] = item
    return items, slot_of, landed, after


ITEMS, SLOT, LANDED, AFTER = plan_loads()
EARLY = [("mod", 0, 0, k) for k in range(N_RAW, DK)]
MOD_ITEMS = ITEMS[:N_RAW] + EARLY + [x for x in ITEMS[N_RAW:] if x[0] == "mod"]
MOD_NO = {x: n for n, x in enumerate(MOD_ITEMS)}
LO_NO = {}
for _e in ("pool", "dve"):
    for _n, _m in enumerate([(l, i) for l in range(DEPTH) for i in range(NB) if lo_engine(i) == _e]):
        LO_NO[_m] = _n


UNIT_OF = [(l, i, n) for l in range(DEPTH) for i in range(NB) if NAMES[i][0] != "fo" for n in range(N_UNITS.get(NAMES[i][0], 1))]
N_ROWS = 13


class Steps:

    def __init__(self, sem):
        self.sem, self.n = sem, 0

    def __call__(self, ins):
        self.n += 1
        ins.then_inc(self.sem, 1)
        return self.n


def trunk(nc, A, out):
    with ExitStack() as ctx:
        def sb(name, shape, dt=F32):
            return ctx.enter_context(nc.sbuf_tensor(name, shape, dt))

        def sem(name):
            return ctx.enter_context(nc.semaphore(name))

        bank = [ctx.enter_context(nc.psum_tensor(f"bank{n}", [P, 512], F32)) for n in range(8)]
        b_mod, b_y = bank[2], bank[3]
        b_bu = [bank[4], bank[5]]
        b_s, b_t = bank[6], bank[7]

        raw = [sb(f"raw{n}", [P, 2048]) for n in range(N_RAW)]
        whi = [sb(f"whi{n}", [P, 2048], F32R) for n in range(N_HI)]
        wlo = [sb(f"wlo{n}", [P, 2048], F32R) for n in range(N_LO)]
        x = sb("x", [P, DK, T])
        h = sb("h", [P, DK, T])
        hhi = sb("hhi", [P, DK, T], F32R)
        hlo = sb("hlo", [P, DK, T], F32R)
        gate = sb("gate", [P, DK, T])
        bhi = sb("bhi", [P, 4, T], F32R)
        blo = sb("blo", [P, 4, T], F32R)
        ctab = sb("ctab", [P, ST, T])
        stab = sb("stab", [P, ST, T])
        m = sb("m", [P, 4, T])
        prod = [sb(f"prod{n}", [P, 4, T]) for n in range(2)]
        u_ssm = sb("u_ssm", [P, CT, T])
        ys = u_ssm
        uc = sb("uc", [P, CT, PAD + T])
        yc = sb("yc", [P, CT, T])
        qT = h[:, 0:4, :]
        kT = sb("kT", [P, T])
        vv = sb("vv", [P, 3, P])
        rtmp = m[:, 0:2, :]
        pr = h[:, 4:6, :].rearrange("p a b -> p (a b)").rearrange("p (t k) -> p t k", t=4)
        pT = h[:, 6:8, :].rearrange("p a b -> p (a b)").rearrange("p (t k) -> p t k", t=4)
        tmp = sb("tmp", [P, 2, T])
        rinv = sb("rinv", [P, T])
        vT = mean = rinv
        modrow = sb("modrow", [P, 512])
        cosr = sb("cosr", [P, T])
        sinr = sb("sinr", [P, T])
        iota = sb("iota", [P, T])
        ident = sb("ident", [P, P])
        ones = sb("ones", [P, P])
        rot = sb("rot", [P, P])
        consts = sb("consts", [P, 16])
        rows = prod[1][:, 0, 0:P]
        ldt = sb("ldt", [ST, 2])
        ldtr = prod[1][0:ST, 0, P:2 * P]
        taps = prod[0][0:TAPS, 0:2, :].rearrange("p a b -> p (a b)")
        vec = [sb(f"vec{l}", [P, P]) for l in range(DEPTH)]
        ldv = [sb(f"ldv{l}", [P, ST]) for l in range(DEPTH)]
        tapv = [sb(f"tapv{l}", [P, CT, TAPS]) for l in range(DEPTH)]
        sink = sb("sink", [P, DEPTH, NQ])
        modv = sb("modv", [P, 48])
        scale1 = sb("scale1", [P, DK])
        scale2 = sb("scale2", [P, DK])
        cact = sb("cact", [P, DK])
        cact32 = sb("cact32", [P, DK, 32])
        small = sb("small", [P, 18, ST])
        bn = yc[:, 0:2, :].rearrange("p a (s i) -> p a s i", i=GROUP)
        cn = yc[:, 2:4, :].rearrange("p a (s n) -> p a s n", n=HEAD)
        uc_flat = uc[:, :, :].rearrange("p c t -> p (c t)")
        bt = uc_flat[:, 0:512].rearrange("p (a s i) -> p a s i", a=2, i=GROUP)
        bsrc = uc_flat[:, 512:1024].rearrange("p (s i) -> p s i", i=2 * GROUP)
        csrc = prod[1][:, 2:4, :].rearrange("p a b -> p (a b)").rearrange("p (c n) -> p c n", c=CT)
        bl = sb("bl", [P, 2, CT, P])
        cl = sb("cl", [P, 3, CT, P])
        rt = sb("rt", [P, 2])
        unused = sb("unused", [P, 1])
        mx = sb("mx", [P, 4])
        nmx = sb("nmx", [P, 4])
        den = sb("den", [P, 4])
        esink = sb("esink", [P, 4])
        rden = sb("rden", [P, 4])
        posi = modrow[:, 0:T].bitcast(I32)

        s_const, s_const2, s_bc, s_x = sem("const_landed"), sem("late_const_landed"), sem("bc_landed"), sem("x_landed")
        s_rows = [sem(f"rows_landed{l}") for l in range(DEPTH)]
        s_land = [sem(f"raw_landed{n}") for n in range(N_RAW)]
        s_early = [sem(f"early_landed{n}") for n in range(len(EARLY))]
        s_hi, s_unit, s_modused = sem("hi_ready"), sem("unit_ready"), sem("mod_weights_used")
        s_lo = {"pool": sem("lo_ready_pool"), "dve": sem("lo_ready_dve")}
        s_dve, s_act = sem("dve_step"), sem("act_step")
        s_out = sem("out_stored")
        ldt_spread, vec_tr, vec_cp, x_tr, x_cp, silu_c, c_ready = (
            sem(n) for n in "ldt_spread vec_tr vec_cp x_tr x_cp silu_c c_ready".split())
        mod_row, mod_tr, mod_ready = (
            sem(n) for n in "mod_row mod_tr mod_ready".split())
        sq_ready, stat_ready, rms_ready, h_ready, hhi_ready, hlo_ready = (
            sem(n) for n in "sq_ready stat_ready rms_ready h_ready hhi_ready hlo_ready".split())
        diag_ready, rinv_ready = sem("diag_ready"), sem("rinv_ready")
        u_ready, bu_ready, bu_used, prod_ready, y_ready, y_used, ys_hi, ys_lo = (
            sem(n) for n in "u_ready bu_ready bu_used prod_ready y_ready y_used ys_hi ys_lo".split())
        qk_ready, rot_ready, rope_ready, vt_ready, v_ready = (
            sem(n) for n in "qk_ready rot_ready rope_ready vt_ready v_ready".split())
        sc_ready, mx_ready, ex_ready, pr_ready, pt_ready, pt_copied, pv_ready, at_hi, at_lo = (
            sem(n) for n in "sc_ready mx_ready ex_ready pr_ready pt_ready pt_copied pv_ready at_hi at_lo".split())
        sigb_ready, uc_ready, conv_ready, csum_ready, mean_ready, cent_ready, csq_ready, cvar_ready, cstd_ready, cnorm_ready, csilu_ready, c_hi, c_lo = (
            sem(n) for n in "sigb_ready uc_ready conv_ready csum_ready mean_ready cent_ready csq_ready cvar_ready cstd_ready cnorm_ready csilu_ready c_hi c_lo".split())
        gate_ready, ao_read, cp_read, glsig_ready, gl_read = (
            sem(n) for n in "gate_ready ao_read cp_read glsig_ready gl_read".split())
        x_mid, x_next, silu_ready, act_ready, act_hi, act_lo, ffn_sum = (
            sem(n) for n in "x_mid x_next silu_ready act_ready act_hi act_lo ffn_sum".split())
        prep_exp, prep_ang, prep_mag, prep_arg, prep_sin, bc_src, bc_tr, bc_cp = (
            sem(n) for n in "prep_exp prep_ang prep_mag prep_arg prep_sin bc_src bc_tr bc_cp".split())
        rope_ang, rope_sin, tab_ang, tab_sin, tab_ready = (
            sem(n) for n in "rope_ang rope_sin tab_ang tab_sin tab_ready".split())
        fin_ready, fin_tr, rt_ready, fin_act, fin_dve = (
            sem(n) for n in "fin_ready fin_tr rt_ready fin_act fin_dve".split())

        w_in, w_ffn_in = A["w_in"], A["w_ffn_in"]

        def by_k(w, l):
            return w[l].rearrange("(k p) n -> p k n", p=P)

        early = [gate[:, :, :], stab[:, 0:DK, :], ctab[:, DK:2 * DK, :], stab[:, DK:2 * DK, :]]
        early = [b.rearrange("p a b -> p (a b)") for b in early]

        def landed_in(item):
            if item in EARLY:
                return early[EARLY.index(item)], s_early[EARLY.index(item)], 16
            return raw[SLOT[item]][:, :], s_land[SLOT[item]], LANDED[item]

        block = ctx.enter_context(nc.Block())

        def small_vectors(eng, l):
            for r0, n, name in ((R_BMOD, 48, "b_mod"), (R_N1, 8, "norm1_g"), (R_N2, 8, "norm2_g"), (R_DWB, 4, "conv_dw_b"),
                                (R_LNG, 4, "conv_ln_g"), (R_LNB, 4, "conv_ln_b"), (R_D, 4, "ssm_d")):
                eng.dma_start(rows[r0:r0 + n, :], A[name][l].rearrange("(r c) -> r c", c=P)).then_inc(s_rows[l], 16)
            for r0, name in ((R_ARE, "ssm_a_re"), (R_AIM, "ssm_a_im")):
                eng.dma_start(rows[r0:r0 + ST, :], A[name][l].rearrange("(s g) n -> s (g n)", g=2)).then_inc(s_rows[l], 16)
            eng.dma_start(rows[R_FIN:R_FIN + DK, :], A["final_norm_g"].rearrange("(r c) -> r c", c=P)).then_inc(s_rows[l], 16)
            eng.dma_start(rows[R_C:R_C + DK, :], A["c"].rearrange("b (r c) -> (b r) c", c=P)).then_inc(s_rows[l], 16)
            eng.dma_start(ldt[:, :], A["ssm_log_dt"][l].rearrange("(s g) -> s g", g=2)).then_inc(s_rows[l], 16)
            eng.dma_start(taps, A["conv_dw_w"][l]).then_inc(s_rows[l], 16)

        def b_and_c(eng, l):
            for c, name in enumerate(("ssm_b_re", "ssm_b_im")):
                eng.dma_start(bn[:, c], A[name][l].rearrange("g n i -> (g n) i").rearrange("(s p) i -> p s i", p=P)).then_inc(s_bc, 16)
            for c, name in enumerate(("ssm_c_re", "ssm_c_im")):
                eng.dma_start(cn[:, c], A[name][l].rearrange("g o n -> (g o) n").rearrange("(s p) n -> p s n", p=P)).then_inc(s_bc, 16)

        def load_x(eng):
            for j in range(2):
                eng.dma_start(h[:, 4 * j:4 * j + 4, :].rearrange("p a b -> p (a b)"), A["x"][0, j * P:(j + 1) * P, :]).then_inc(s_x, 16)

        def late_constants(eng):
            eng.dma_start(ones[:, :], A["c_ones"]).then_inc(s_const2, 16)
            eng.dma_start(rot[:, :], A["c_rot"]).then_inc(s_const2, 16)
            eng.dma_start(iota[:, :], A["c_iota"]).then_inc(s_const2, 16)
            eng.dma_start(posi, A["positions"].to_broadcast([P, T])).then_inc(s_const2, 16)
            eng.dma_start(sink[:, :, :], A["attn_sinks"].rearrange("(o l) q -> o l q", o=1).to_broadcast([P, DEPTH, NQ])).then_inc(s_const2, 16)

        @block.sync
        def _(sp):
            sp.dma_start(ident[:, :], A["c_ident"]).then_inc(s_const, 16)
            sp.dma_start(consts[:, :], A["c_small"]).then_inc(s_const, 16)

            def main(l, i, dst):
                kind, n = NAMES[i]
                k8 = dst.rearrange("p (k n) -> p k n", k=DK)
                k4 = dst.rearrange("p (k n) -> p k n", k=4)
                if kind in ("su", "ca", "cb", "ga", "gc", "gs", "kv"):
                    c0 = {"su": OFF_SU, "ca": OFF_CA, "cb": OFF_CB, "ga": OFF_G, "gc": OFF_G + D, "gs": OFF_G + 2 * D, "kv": OFF_K}[kind] + BC * n
                    return [(k8, by_k(w_in, l)[:, :, c0:c0 + BC])]
                if kind == "q":
                    return [(k8[:, :, c * P + g * HEAD:c * P + (g + 1) * HEAD],
                             by_k(w_in, l)[:, :, g * 256 + (2 * n + c) * HEAD:g * 256 + (2 * n + c + 1) * HEAD]) for c in range(2) for g in range(NKV)]
                if kind == "ao":
                    w = A["w_attn_o"][l].rearrange("(g t d) n -> g d t n", g=NKV, d=HEAD)
                    return [(k4[g * HEAD:(g + 1) * HEAD], w[g][:, :, n * 512:(n + 1) * 512]) for g in range(NKV)]
                if kind in ("cp", "gla", "glb"):
                    w = A[{"cp": "conv_pw_w", "gla": "ssm_glu_a", "glb": "ssm_glu_b"}[kind]]
                    return [(k4, by_k(w, l)[:, :, n * 512:(n + 1) * 512])]
                if kind == "wo":
                    return [(k8, by_k(A["w_out"], l)[:, :, n * BC:(n + 1) * BC])]
                if kind in ("fg", "fu"):
                    c0 = n * BC + (DFF if kind == "fu" else 0)
                    return [(k8, by_k(w_ffn_in, l)[:, :, c0:c0 + BC])]
                return [(dst.rearrange("p (k n) -> p k n", k=2), by_k(A["w_ffn_out"], l)[:, 2 * n:2 * n + 2, :])]

            for n, item in enumerate(ITEMS[:N_RAW] + EARLY[:-1] + ITEMS[N_RAW:N_RAW + 1] + EARLY[-1:] + ITEMS[N_RAW + 1:]):
                if n == 1:
                    small_vectors(sp, 0)
                was = AFTER.get(item)
                if was and was[0] == "main":
                    e = lo_engine(was[2])
                    sp.wait_ge(s_lo[e], LO_NO[(was[1], was[2])] + 1)
                elif was:
                    sp.wait_ge(s_modused, MOD_NO[was] + 1)
                dst, landed, _ = landed_in(item)
                if item[0] == "mod":
                    _, l, ng, k = item
                    sp.dma_start(dst, A["w_mod"][l, k * P:(k + 1) * P, ng * MODC:(ng + 1) * MODC]).then_inc(landed, 16)
                else:
                    if item[1:] == (0, PREP_AT) and DEPTH > 1:
                        sp.wait_ge(gl_read, 4)
                        small_vectors(sp, 1)
                    for d, src in main(item[1], item[2], dst):
                        sp.dma_start(d, src).then_inc(landed, 16)
                    if item[1] == 0 and DEPTH > 1 and item[2] == AT[("wo", 0)]:
                        sp.wait_ge(bc_src, 4)
                        b_and_c(sp, 1)
            for n in range(4):
                j, c = divmod(n, 2)
                sp.wait_ge((fin_act, fin_dve)[c], j + 1)
                sp.dma_start(out[0, j * P:(j + 1) * P, c * 512:(c + 1) * 512],
                             h[:, 2 * n:2 * n + 2, :].rearrange("p a b -> p (a b)")).then_inc(s_out, 16)
            sp.wait_ge(s_out, 64)

        @block.tensor
        def _(pe):
            mm = nc.tensor.matmul

            def hi_lo(o, w_hi, w_lo, a_hi, a_lo, start, stop):
                mm(o, w_hi, a_hi, start=start, stop=False, skip_group_check=True)
                mm(o, w_hi, a_lo, start=False, stop=False, skip_group_check=True)
                return mm(o, w_lo, a_hi, start=False, stop=stop, skip_group_check=True)

            def unit_bank(l, i, n=0):
                b = l * BANKS + BANK0[i] + n
                if b >= 2:
                    pl, pi, pn = UNIT_OF[b - 2]
                    kind, kn = NAMES[pi]
                    done, value = {
                        "su": (u_ready, 2 * pl + kn + 1), "q": (qk_ready, 3 * pl + kn + 1),
                        "kv": (qk_ready, 3 * pl + 3),
                        "cb": (sigb_ready, 2 * pl + kn + 1), "ca": (uc_ready, 2 * pl + kn + 1),
                        "ga": (gate_ready, 12 * pl + kn + 1), "gc": (gate_ready, 12 * pl + 5 + kn), "gs": (gate_ready, 12 * pl + 9 + kn),
                        "ao": (ao_read, 4 * pl + 2 * kn + pn + 1), "cp": (cp_read, 4 * pl + 2 * kn + pn + 1),
                        "glb": (glsig_ready, 4 * pl + 2 * kn + pn + 1), "gla": (gl_read, 4 * pl + 2 * kn + pn + 1),
                        "wo": (x_mid, 4 * pl + kn + 1), "fg": (silu_ready, NF * pl + kn + 1), "fu": (act_ready, NF * pl + kn + 1),
                    }[kind]
                    pe.wait_ge(done, value)
                return bank[b % 2]

            def mod_block(l, ng, k):
                item = ("mod", l, ng, k)
                weights, landed, value = landed_in(item)
                pe.wait_ge(landed, value)
                if MOD_NO[item] == 0:
                    pe.wait_ge(c_ready, 1)
                elif k == 0:
                    pe.wait_ge(mod_ready, MOD_NO[item] // DK)
                    if ng == (2 if l else 1):
                        pe.wait_ge(v_ready, l + 1)
                for q in range(4):
                    last = mm(b_mod[32 * q:32 * q + 32, :], cact32[:, k, :], weights[:, q * 512:(q + 1) * 512],
                              start=(k == 0), stop=(k == DK - 1), skip_group_check=True)
                last.then_inc(s_modused, 1)

            def mod_columns(n):
                pe.wait_ge(mod_row, n + 1)
                for j in range(4):
                    last = mm(b_mod[:, 4 * j:4 * j + 4], modrow[:, j * P:(j + 1) * P], consts[:, 0:4], start=(j == 0), stop=(j == 3), skip_group_check=True)
                last.then_inc(mod_tr, 1)

            def mean_square(n, c):
                if c == 0 and n == 0:
                    pe.wait_ge(vec_cp, 1)
                    pe.wait_ge(s_const2, 16 * 5)
                elif c == 0 and n % 2:
                    pe.wait_ge(y_used, n + 1)
                elif c == 0 and n < 2 * DEPTH:
                    pe.wait_ge(bc_cp, 4 * (n // 2 + 1))
                pe.wait_ge(sq_ready, 4 * n + c + 1)
                for k in (2 * c, 2 * c + 1):
                    for j in range(2):
                        last = mm(b_y[:, j:j + 1], h[:, k, j * P:(j + 1) * P], ones[:, 0:1], start=(k == 0 and j == 0), stop=(k == DK - 1), skip_group_check=True)
                if c == 3:
                    last.then_inc(stat_ready, 1)

            def spread(n):
                pe.wait_ge(diag_ready, n + 1)
                mm(b_y[:, T:2 * T], ones[:, :], rinv[:, :], start=True, stop=True, skip_group_check=True).then_inc(rinv_ready, 1)

            def ssm_in(l, pair):
                n = l * ST + 2 * pair
                pe.wait_ge(u_ready, 2 * l + pair // 4 + 1)
                if pair == 0:
                    pe.wait_ge(bc_cp, 4 * (l + 1))
                if n:
                    pe.wait_ge(bu_used, n)
                for c in range(2):
                    for t in (2 * pair, 2 * pair + 1):
                        r = 32 * (t % 4)
                        last = mm(b_bu[t % 2][:, c * T:(c + 1) * T], bl[r:r + 32, c, t // 4, :], u_ssm[r:r + 32, t // 4, :], start=True, stop=True)
                        if c == 1:
                            last.then_inc(bu_ready, 1)

            def ssm_out(l, pair):
                n = l * ST + 2 * pair
                pe.wait_ge(prod_ready, n + 2)
                if n and pair % 4 == 0:
                    pe.wait_ge(y_used, n // 8)
                if pair == 0:
                    pe.wait_ge(h_ready, H_PER_LAYER * l + DK)
                for c, w in enumerate((0, 2, 2, 1)):
                    for t in (2 * pair, 2 * pair + 1):
                        r = 32 * (t % 4)
                        half = (t // 4) % 2
                        last = mm(b_y[r:r + 32, half * T:(half + 1) * T], cl[:, w, t // 4, r:r + 32], prod[t % 2][:, c, :],
                                  start=(c == 0), stop=(c == 3), skip_group_check=True)
                        if c == 3:
                            last.then_inc(y_ready, 1)

            def rotate(l, c):
                pe.wait_ge(qk_ready, 3 * l + c + 1)
                if c == 2:
                    pe.wait_ge(rope_ready, 3 * l + 1)
                o = (b_s, b_t, b_s)[c]
                for j in range(2 if c < 2 else 1):
                    src = qT[:, 2 * c + j, :] if c < 2 else kT[:, :]
                    last = mm(o[:, j * T:(j + 1) * T], rot[:, :], src, start=(j == 0), stop=True, skip_group_check=True)
                last.then_inc(rot_ready, 1)

            def v_transposes(l):
                for c, t0 in enumerate((0, CHUNK, P)):
                    last = nc.tensor.transpose(b_mod[:, c * P:(c + 1) * P], vT[:, t0:t0 + P], ident[:, :])
                last.then_inc(vt_ready, 1)

            def scores(l, r):
                n = 4 * l + r
                j, g = divmod(r, 2)
                p = slice(g * HEAD, (g + 1) * HEAD)
                if r == 0:
                    pe.wait_ge(rope_ready, 3 * l + 3)
                else:
                    pe.wait_ge(ex_ready, n)
                for t in range(4):
                    o = b_s[:, t * KEYS:(t + 1) * KEYS]
                    if j == 0:
                        last = mm(o, qT[p, t, 0:P], kT[p, 0:P], start=(t == 0), stop=(t == 3), skip_group_check=True)
                    else:
                        for c in range(2):
                            last = mm(o[c * CHUNK:(c + 1) * CHUNK, :], qT[p, t, P + c * CHUNK:P + (c + 1) * CHUNK],
                                      kT[p, CHUNK * (c + 1):CHUNK * (c + 1) + KEYS], start=(t == 0), stop=(t == 3), skip_group_check=True)
                last.then_inc(sc_ready, 1)

            def probs_t(l, r):
                n = 4 * l + r
                pe.wait_ge(pr_ready, n + 1)
                if r == 0:
                    pe.wait_ge(v_ready, l + 1)
                else:
                    pe.wait_ge(at_lo, n)
                for t in range(4):
                    last = nc.tensor.transpose(b_t[:, t * P:(t + 1) * P], pr[:, t, :], ident[:, :])
                last.then_inc(pt_ready, 1)

            def attend(l, r):
                n = 4 * l + r
                j, g = divmod(r, 2)
                p = slice(g * HEAD, (g + 1) * HEAD)
                pe.wait_ge(pt_copied, n + 1)
                o = b_t[p, :].rearrange("p (t q) -> p t q", t=4)
                if j == 0:
                    last = mm(o, vv[:, 0, p], pT[:, :, :], start=True, stop=True)
                else:
                    for c in range(2):
                        last = mm(o[:, :, c * CHUNK:(c + 1) * CHUNK], vv[:, 1 + c, p], pT[:, :, c * CHUNK:(c + 1) * CHUNK],
                                  start=(c == 0), stop=(c == 1), skip_group_check=True)
                last.then_inc(pv_ready, 1)

            def conv_stat(l, n):
                if n == 0:
                    pe.wait_ge(at_lo, 4 * (l + 1))
                pe.wait_ge(conv_ready if n == 0 else csq_ready, l + 1)
                src = yc[:, :, :] if n == 0 else uc[:, :, 0:T]
                for c in range(CT):
                    last = mm(b_t[:, n * T:(n + 1) * T], ones[:, :], src[:, c, :], start=(c == 0), stop=(c == CT - 1), skip_group_check=True)
                last.then_inc(csum_ready if n == 0 else cvar_ready, 1)

            def bc_transposes(l, n):
                pe.wait_ge(bc_src, 4 * l + n + 1)
                if n:
                    pe.wait_ge(bc_cp, 4 * l + n)
                    if (l, n) == (0, 3):
                        pe.wait_ge(h_ready, DK)
                elif l:
                    pe.wait_ge(vec_cp, l + 1)
                else:
                    pe.wait_ge(rms_ready, 1)
                for c in range(CT):
                    src = bsrc[:, 4 * c:4 * c + 4, :].rearrange("p a b -> p (a b)") if n < 2 else csrc[:, c, :]
                    last = nc.tensor.transpose(b_y[:, c * P:(c + 1) * P], src, ident[:, :])
                last.then_inc(bc_tr, 1)

            def main_block(l, i, middle):
                kind, n = NAMES[i]
                mi = l * NB + i
                W, V = whi[mi % N_HI], wlo[mi % N_LO]
                pe.wait_ge(s_lo[lo_engine(i)], LO_NO[(l, i)] + 1)
                w8 = [w[:, :].rearrange("p (k n) -> p k n", k=DK) for w in (W, V)]
                w4 = [w[:, :].rearrange("p (k n) -> p k n", k=4) for w in (W, V)]
                if n == 0 and kind in ("su", "wo", "fg"):
                    o = unit_bank(l, i)
                    for k in range(DK):
                        done = H_PER_LAYER * l + H0[kind] + (k // 2 if kind == "wo" else k) + 1
                        pe.wait_ge(hlo_ready, done)
                        for c in range(2):
                            last = hi_lo(o[:, c * T:(c + 1) * T], w8[0][:, k, c * P:(c + 1) * P], w8[1][:, k, c * P:(c + 1) * P], hhi[:, k, :], hlo[:, k, :],
                                         k == 0 and c == 0, k == DK - 1)
                    last.then_inc(s_unit, 1)
                elif kind in ("ao", "cp", "gla", "glb"):
                    if n == 0 and kind != "gla":
                        pe.wait_ge({"ao": at_lo, "cp": c_lo, "glb": ys_lo}[kind], {"ao": 4 * (l + 1), "cp": l + 1, "glb": l + 1}[kind])
                    for half in range(2):
                        o = unit_bank(l, i, half)
                        for c in range(2):
                            cols = slice((2 * half + c) * P, (2 * half + c + 1) * P)
                            for k in range(4):
                                last = hi_lo(o[:, c * T:(c + 1) * T], w4[0][:, k, cols], w4[1][:, k, cols], bhi[:, k, :], blo[:, k, :], k == 0, k == 3)
                        last.then_inc(s_unit, 1)
                        if half == 0:
                            middle()
                elif kind == "fo":
                    w2 = [w[:, :].rearrange("p (k n) -> p k n", k=2) for w in (W, V)]
                    pe.wait_ge(act_lo, l * NF + n + 1)
                    if n == 0:
                        pe.wait_ge(cstd_ready, l + 1)
                    for c in range(DK):
                        o = bank[4 + c // 2][:, (c % 2) * T:(c % 2 + 1) * T]
                        for k in range(2):
                            a = (n % 2) * 2 + k
                            last = hi_lo(o, w2[0][:, k, c * P:(c + 1) * P], w2[1][:, k, c * P:(c + 1) * P], bhi[:, a, :], blo[:, a, :],
                                         n == 0 and k == 0 and c % 2 == 0, n == NF - 1 and k == 1)
                        if n == NF - 1 and c % 2 and c < DK - 1:
                            last.then_inc(ffn_sum, 1)
                        if n == NF - 1 and c in (5, 6):
                            mean_square(2 * l + 2, c - 5)
                        if c == 3:
                            middle()
                    last.then_inc(s_unit, 1)
                else:
                    o = unit_bank(l, i)
                    for c in range(2):
                        for k in range(DK):
                            st = [w[:, k, c * P:(c + 1) * P] for w in w8]
                            last = hi_lo(o[:, c * T:(c + 1) * T], st[0], st[1], hhi[:, k, :], hlo[:, k, :], k == 0, k == DK - 1)
                        if c == 0:
                            middle()
                    last.then_inc(s_unit, 1)

            def small_columns(l):
                pe.wait_ge(s_rows[l], 16 * N_ROWS)
                pe.wait_ge(ldt_spread, l + 1)
                if l:
                    pe.wait_ge(h_ready, H_PER_LAYER * l)
                nc.tensor.transpose(b_y[:, 0:P], rows, ident[:, :])
                nc.tensor.transpose(b_y[:, P:P + ST], ldtr, ident[0:ST, 0:ST])
                for c in range(CT):
                    last = nc.tensor.transpose(b_y[:, 256 + c * 32:256 + c * 32 + TAPS], taps[:, c * P:(c + 1) * P], ident[0:TAPS, 0:TAPS])
                last.then_inc(vec_tr, 1)

            def side(l, t):
                if t == ROPE_Q_AT:
                    rotate(l, 0)
                    rotate(l, 1)
                if t == ROPE_K_AT:
                    rotate(l, 2)
                    v_transposes(l)
                if t in PROBS_AT:
                    probs_t(l, PROBS_AT[t])
                if t in ATTEND_AT:
                    attend(l, ATTEND_AT[t])
                if t in SCORES_AT:
                    scores(l, SCORES_AT[t])
                if t in SSM_OUT_AT:
                    ssm_out(l, SSM_OUT_AT[t])
                if t in SSM_IN_AT:
                    ssm_in(l, SSM_IN_AT[t])
                if t in MEAN_SQUARE_AT:
                    mean_square(2 * l + 1, MEAN_SQUARE_AT[t])
                if t in (CONV_MEAN_AT, CONV_VAR_AT):
                    conv_stat(l, int(t == CONV_VAR_AT))

            pe.wait_ge(s_const, 32)
            small_columns(0)
            for k in range(DK):
                mod_block(0, 0, k)
                if k == 1:
                    pe.wait_ge(s_x, 32)
                    for c in range(DK):
                        for j in range(2):
                            last = nc.tensor.transpose(bank[4 + c // 2][:, (c % 2) * T + j * P:(c % 2) * T + (j + 1) * P],
                                                       h[:, 4 * j + c // 2, (c % 2) * P:(c % 2 + 1) * P], ident[:, :])
                        if c % 2:
                            last.then_inc(x_tr, 1)
                if k == 2:
                    for c in range(4):
                        mean_square(0, c)
                if 4 <= k < 7:
                    bc_transposes(0, k - 4)
            mod_columns(0)
            spread(0)

            def behind_norm(l, i):
                n = 2 * l + (NAMES[i][0] == "fg")
                mods = mods_at(l, i)
                if n:
                    if n % 2 == 0:
                        mean_square(n, 2)
                    for m3 in mods:
                        mod_block(*m3)
                    mean_square(n, 3)
                    spread(n)

            for l in range(DEPTH):
                for i in range(NB):
                    for n in mod_ends_at(l, i - 2):
                        mod_columns(n)
                    if NAMES[i] in (("su", 0), ("fg", 0)):
                        behind_norm(l, i)
                    else:
                        for m3 in mods_at(l, i):
                            mod_block(*m3)
                    side(l, 2 * i)
                    if (l, i) == (0, 1):
                        bc_transposes(0, 3)
                    if i == PREP_AT - 1 and l + 1 < DEPTH:
                        small_columns(l + 1)
                    if l + 1 < DEPTH and i in BC_TR_AT:
                        bc_transposes(l + 1, BC_TR_AT[i])
                    main_block(l, i, lambda: side(l, 2 * i + 1))
            mean_square(2 * DEPTH, 2)
            for n in range(4):
                j, c = divmod(n, 2)
                for k in range(4 * c, 4 * c + 4):
                    pe.wait_ge(fin_ready, k + 1)
                    last = nc.tensor.transpose(bank[4 + n][:, (k % 4) * P:(k % 4 + 1) * P], gate[:, k, j * P:(j + 1) * P], ident[:, :])
                last.then_inc(fin_tr, 1)
                if n == 1:
                    mean_square(2 * DEPTH, 3)

        @block.gpsimd
        def _(pool):
            for l in range(DEPTH):
                for i in range(NB):
                    if lo_engine(i) != "pool":
                        continue
                    mi = l * NB + i
                    pool.wait_ge(s_hi, mi + 1)
                    if mi >= N_LO:
                        pool.wait_ge(s_unit, used(mi - N_LO))
                    nc.gpsimd.tensor_tensor(wlo[mi % N_LO][:, :], raw[SLOT[("main", l, i)]][:, :], whi[mi % N_HI][:, :].bitcast(F32),
                                            ALU.subtract).then_inc(s_lo["pool"], 1)

        @block.scalar
        def _(act):
            step = Steps(s_act)
            fn = nc.scalar.activation

            def halves(ap):
                return ap.rearrange("p (c t) -> p c t", c=2)

            def hi(mi):
                if mi >= DEPTH * NB:
                    return
                item = ("main", *divmod(mi, NB))
                act.wait_ge(s_land[SLOT[item]], LANDED[item])
                if mi >= N_HI:
                    act.wait_ge(s_unit, used(mi - N_HI))
                fn(whi[mi % N_HI][:, :], raw[SLOT[item]][:, :], ACT.Copy).then_inc(s_hi, 1)

            def unit(l, i, n=0):
                act.wait_ge(s_unit, l * UNITS + UNIT0[i] + n + 1)
                return bank[(l * BANKS + BANK0[i] + n) % 2][:, :]

            def squares(n, c):
                if n == 0:
                    act.wait_ge(x_cp, 4)
                elif n % 2:
                    act.wait_ge(x_mid, 4 * (n // 2) + c + 1)
                    act.wait_ge(hlo_ready, H_PER_LAYER * (n // 2) + H0["fg"])
                else:
                    act.wait_ge(x_next, 4 * (n // 2 - 1) + c + 1)
                fn(h[:, 2 * c:2 * c + 2, :], x[:, 2 * c:2 * c + 2, :], ACT.Square).then_inc(sq_ready, 1)

            def norm(n):
                if n == 0:
                    for c in range(4):
                        squares(n, c)
                act.wait_ge(stat_ready, n + 1)
                fn(rt[:, :], b_y[:, 0:2], ACT.Sqrt, bias=consts[:, 7:8], scale=1.0 / D).then_inc(rms_ready, 1)

            def norm_hi(l, kind, shift, k0, k1):
                for k in range(k0, k1):
                    act.wait_ge(h_ready, H_PER_LAYER * l + H0[kind] + k + 1)
                    fn(hhi[:, k, :], h[:, k, :], ACT.Identity, bias=modv[:, shift + k:shift + k + 1]).then_inc(hhi_ready, 1)

            def mix_hi(l, c):
                act.wait_ge(h_ready, H_PER_LAYER * l + H0["wo"] + c + 1)
                fn(hhi[:, 2 * c:2 * c + 2, :], h[:, 2 * c:2 * c + 2, :], ACT.Copy).then_inc(hhi_ready, 1)

            def mod_copy(n):
                act.wait_ge(s_modused, DK * (n + 1))
                if n:
                    act.wait_ge(mod_tr, n)
                fn(modrow[:, :], b_mod[:, :], ACT.Copy).then_inc(mod_row, 1)

            def prep(l):
                act.wait_ge(vec_cp, l + 1)
                fn(small[:, 0, :], ldv[l][:, :], ACT.Exp).then_inc(prep_exp, 1)
                act.wait_ge(prep_ang, l + 1)
                fn(small[:, 3, :], small[:, 2, :], ACT.Exp).then_inc(prep_mag, 1)
                act.wait_ge(prep_arg, l + 1)
                fn(small[:, 6, :], small[:, 5, :], ACT.Sin)
                fn(small[:, 7, :], small[:, 5, :], ACT.Sin, scale=0.5).then_inc(prep_sin, 1)

            def bc_copy(l, n):
                act.wait_ge(bc_tr, 4 * l + n + 1)
                src = b_y[:, :].rearrange("p (c s) -> p c s", c=CT)
                if n < 2:
                    fn(bl[:, n], src, ACT.Copy).then_inc(bc_cp, 1)
                elif n == 2:
                    fn(cl[:, 0], src, ACT.Copy)
                    fn(cl[:, 1], src, ACT.Copy, scale=-1.0).then_inc(bc_cp, 1)
                else:
                    fn(cl[:, 2], src, ACT.Copy, scale=-1.0).then_inc(bc_cp, 1)

            def table(l, n):
                q = slice(4 * n, 4 * n + 4)
                act.wait_ge(tab_ang, 4 * l + n + 1)
                fn(stab[:, q, :], m[:, :, :], ACT.Sin, scale=2 * PI_LOW)
                fn(ctab[:, q, :], m[:, :, :], ACT.Sin, scale=PI_LOW).then_inc(tab_sin, 1)
                act.wait_ge(tab_sin, 4 * l + n + 1)
                act.wait_ge(s_act, step(fn(ctab[:, q, :], ctab[:, q, :], ACT.Square)))
                fn(ctab[:, q, :], ctab[:, q, :], ACT.Identity, scale=-2.0, bias=ones[:, 0:1]).then_inc(tab_ready, 1)

            def softmax_exp(l, r):
                n = 4 * l + r
                act.wait_ge(mx_ready, n + 1)
                if n:
                    act.wait_ge(pt_ready, n)
                for t in range(4):
                    fn(pr[:, t, :], b_s[:, t * KEYS:(t + 1) * KEYS], ACT.Exp, bias=nmx[:, t:t + 1], scale=HEAD ** -0.5, accum_out=den[:, t:t + 1])
                fn(esink[:, :], esink[:, :], ACT.Exp).then_inc(ex_ready, 1)

            def probs_copy(l, r):
                act.wait_ge(pt_ready, 4 * l + r + 1)
                fn(pT[:, :, :], b_t[:, :].rearrange("p (t q) -> p t q", t=4), ACT.Copy).then_inc(pt_copied, 1)

            def att_hi(l, r):
                j, g = divmod(r, 2)
                p = slice(g * HEAD, (g + 1) * HEAD)
                act.wait_ge(pv_ready, 4 * l + r + 1)
                fn(bhi[p, :, j * P:(j + 1) * P], b_t[p, :].rearrange("p (t q) -> p t q", t=4), ACT.Copy).then_inc(at_hi, 1)

            def conv_mean(l):
                act.wait_ge(csum_ready, l + 1)
                fn(mean[:, :], b_t[:, 0:T], ACT.Copy, scale=1.0 / CW).then_inc(mean_ready, 1)
                act.wait_ge(cent_ready, l + 1)
                fn(uc[:, :, 0:T], yc[:, :, :], ACT.Square).then_inc(csq_ready, 1)

            def conv_silu(l):
                act.wait_ge(cvar_ready, l + 1)
                fn(mean[:, :], b_t[:, T:2 * T], ACT.Sqrt, bias=consts[:, 7:8], scale=1.0 / CW).then_inc(cstd_ready, 1)
                act.wait_ge(cnorm_ready, l + 1)
                for c in range(CT):
                    last = fn(yc[:, c, :], yc[:, c, :], ACT.Silu, scale=vec[l][:, R_LNG + c:R_LNG + c + 1], bias=vec[l][:, R_LNB + c:R_LNB + c + 1])
                last.then_inc(csilu_ready, 1)
                act.wait_ge(csilu_ready, l + 1)
                act.wait_ge(s_unit, used(l * NB + AT[("ao", 1)]))
                fn(bhi[:, :, :], yc[:, :, :], ACT.Copy).then_inc(c_hi, 1)

            def ssm_hi(l):
                act.wait_ge(y_used, 2 * (l + 1))
                act.wait_ge(s_unit, used(l * NB + AT[("cp", 1)]))
                fn(bhi[:, :, :], ys[:, :, :], ACT.Copy).then_inc(ys_hi, 1)

            def post(l, i):
                kind, n = NAMES[i]
                two = slice(2 * n, 2 * n + 2)
                if kind == "su":
                    fn(u_ssm[:, two, :], halves(unit(l, i)), ACT.Copy).then_inc(u_ready, 1)
                elif kind == "q":
                    fn(qT[:, two, :], halves(unit(l, i)), ACT.Copy).then_inc(qk_ready, 1)
                elif kind == "kv":
                    b = unit(l, i)
                    fn(kT[:, :], b[:, 0:T], ACT.Copy)
                    fn(vT[:, :], b[:, T:2 * T], ACT.Copy).then_inc(qk_ready, 1)
                elif kind == "cb":
                    if 2 * l + n:
                        act.wait_ge(uc_ready, 2 * l + n)
                    fn(tmp[:, :, :], halves(unit(l, i)), ACT.Sigmoid).then_inc(sigb_ready, 1)
                elif kind in ("ga", "gc", "gs"):
                    b = unit(l, i)
                    if kind != "ga":
                        act.wait_ge(ao_read if kind == "gc" else cp_read, 4 * l + n + 1)
                    fn(gate[:, two, :], halves(b), ACT.Sigmoid).then_inc(gate_ready, 1)
                elif kind == "glb":
                    for half in range(2):
                        b = unit(l, i, half)
                        if n:
                            act.wait_ge(gl_read, 4 * l + half + 1)
                        fn(prod[half][:, 0:2, :], halves(b), ACT.Sigmoid).then_inc(glsig_ready, 1)
                elif kind == "fg":
                    b = unit(l, i)
                    if n >= 2:
                        act.wait_ge(act_lo, l * NF + n - 1)
                    a = 2 * (n % 2)
                    fn(gate[:, a:a + 2, :], halves(b), ACT.Silu).then_inc(silu_ready, 1)
                elif kind == "wo":
                    squares(2 * l + 1, n)
                elif kind == "fu":
                    act.wait_ge(act_ready, l * NF + n + 1)
                    if n >= 2:
                        act.wait_ge(s_unit, used(l * NB + AT[("fo", n - 2)]))
                    a = 2 * (n % 2)
                    fn(bhi[:, a:a + 2, :], gate[:, a:a + 2, :], ACT.Copy).then_inc(act_hi, 1)

            def side(l, t):
                if t in PROBS_AT:
                    probs_copy(l, PROBS_AT[t])
                if t in ATTEND_AT:
                    att_hi(l, ATTEND_AT[t])
                if t in SCORES_AT:
                    softmax_exp(l, SCORES_AT[t])
                if t == CONV_MEAN_AT:
                    conv_mean(l)
                if t == CONV_VAR_AT:
                    conv_silu(l)
                if t == SSM_SPLIT_AT:
                    ssm_hi(l)

            load_x(act)
            late_constants(act)
            b_and_c(act, 0)
            act.wait_ge(vec_cp, 1)
            fn(cact[:, :], vec[0][:, R_C:R_C + DK], ACT.Silu).then_inc(silu_c, 1)
            prep(0)
            for n in range(4):
                act.wait_ge(x_tr, n + 1)
                fn(x[:, 2 * n:2 * n + 2, :], halves(bank[4 + n][:, :]), ACT.Copy).then_inc(x_cp, 1)
            norm(0)
            for n in range(3):
                bc_copy(0, n)
            hi(0)
            mod_copy(0)
            norm_hi(0, "su", M_SH1, 0, 4)
            hi(1)
            norm_hi(0, "su", M_SH1, 4, DK)
            bc_copy(0, 3)
            for l in range(DEPTH):
                for i in range(NB):
                    side(l, 2 * i)
                    if i in BEFORE_NORM:
                        fn(unused[:, :], consts[:, 7:8], ACT.Sqrt)
                    if i == NB - 1:
                        for c in range(4):
                            squares(2 * l + 2, c)
                    else:
                        hi(l * NB + i + AHEAD)
                    for n in mod_ends_at(l, i):
                        mod_copy(n)
                    side(l, 2 * i + 1)
                    if l + 1 < DEPTH:
                        if i == PREP_AT:
                            prep(l + 1)
                        if i in BC_TR_AT:
                            bc_copy(l + 1, BC_TR_AT[i])
                        if i in TABLE_AT:
                            table(l + 1, TABLE_AT[i])
                    if (l, i) == (0, 1):
                        act.wait_ge(rope_ang, 1)
                        fn(sinr[:, :], tmp[:, 0, :], ACT.Sin)
                        fn(cosr[:, :], tmp[:, 0, :], ACT.Sin, scale=0.5).then_inc(rope_sin, 1)
                    post(l, i)
                    if l == 0 and i in FIRST_TABLE_AT:
                        table(0, FIRST_TABLE_AT[i])
                    if NAMES[i][0] == "gla":
                        for half in range(2):
                            mix_hi(l, 2 * NAMES[i][1] + half)
                    if NAMES[i] == ("wo", 3):
                        norm(2 * l + 1)
                        norm_hi(l, "fg", M_SH2, 0, DK)
                norm(2 * l + 2)
                if l + 1 < DEPTH:
                    norm_hi(l + 1, "su", M_SH1, 0, DK // 2)
                    hi((l + 1) * NB + AHEAD - 1)
                    norm_hi(l + 1, "su", M_SH1, DK // 2, DK)
            for j in range(2):
                act.wait_ge(fin_tr, 2 * j + 1)
                act.wait_ge(rt_ready, 1)
                fn(h[:, 4 * j:4 * j + 2, :], halves(bank[4 + 2 * j][:, :]), ACT.Copy, scale=rt[:, j:j + 1]).then_inc(fin_act, 1)

        @block.vector
        def _(dve):
            step = Steps(s_dve)
            V = nc.vector

            def then(ins):
                dve.wait_ge(s_dve, step(ins))

            def bcast(ap, n):
                return ap.rearrange("p (a o) -> p a o", o=1).to_broadcast([ap.shape[0], ap.shape[1], n])

            def rows4(ap, n):
                return ap.rearrange("p (o t) -> p o t", o=1).to_broadcast([P, n, T])

            def halves(ap):
                return ap.rearrange("p (c t) -> p c t", c=2)

            def lo(mi):
                if mi >= DEPTH * NB or lo_engine(mi % NB) != "dve":
                    return
                dve.wait_ge(s_hi, mi + 1)
                if mi >= N_LO:
                    dve.wait_ge(s_unit, used(mi - N_LO))
                V.tensor_tensor(wlo[mi % N_LO][:, :], raw[SLOT[("main", *divmod(mi, NB))]][:, :], whi[mi % N_HI][:, :].bitcast(F32),
                                ALU.subtract).then_inc(s_lo["dve"], 1)

            def unit(l, i, n=0):
                dve.wait_ge(s_unit, l * UNITS + UNIT0[i] + n + 1)
                return bank[(l * BANKS + BANK0[i] + n) % 2][:, :]

            def reduce_angle(dst, src, k):
                then(V.tensor_scalar(k, src, 1.0 / TWO_PI, ROUND, ALU.mult, ALU.add))
                then(V.tensor_scalar(k, k, ROUND, None, ALU.subtract))
                then(V.scalar_tensor_tensor(out=dst, in0=k, scalar=-C1, in1=src, op0=ALU.mult, op1=ALU.add))
                then(V.scalar_tensor_tensor(out=dst, in0=k, scalar=-C2, in1=dst, op0=ALU.mult, op1=ALU.add))
                then(V.scalar_tensor_tensor(out=dst, in0=k, scalar=-C3, in1=dst, op0=ALU.mult, op1=ALU.add))
                return V.tensor_scalar(dst, dst, PI_LOW, -PI_LOW, ALU.min, ALU.max)

            dt, th, dr, mag, turn, ang, sn, sh, cs, turns, nre, nim, d1, d2, fre, fim, t1, t2 = (small[:, n, :] for n in range(18))
            tt = V.tensor_tensor

            def ssm_a(l):
                return vec[l][:, R_ARE:R_ARE + ST], vec[l][:, R_AIM:R_AIM + ST]

            def discretize(l):
                a_re, a_im = ssm_a(l)
                dve.wait_ge(prep_exp, l + 1)
                tt(dr, dt, a_re, ALU.mult).then_inc(prep_ang, 1)
                then(tt(th, dt, a_im, ALU.mult))
                reduce_angle(ang, th, turn).then_inc(prep_arg, 1)
                dve.wait_ge(prep_arg, l + 1)
                then(V.tensor_scalar(turns, ang, 1.0 / TWO_PI, None, ALU.mult))
                then(tt(d1, a_re, a_re, ALU.mult))
                then(tt(d2, a_im, a_im, ALU.mult))
                then(tt(d1, d1, d2, ALU.add))
                then(V.reciprocal(d2, d1))

            def b_factor(l):
                a_re, a_im = ssm_a(l)
                dve.wait_ge(prep_mag, l + 1)
                dve.wait_ge(prep_sin, l + 1)
                then(tt(cs, sh, sh, ALU.mult))
                then(V.tensor_scalar(cs, cs, -2.0, 1.0, ALU.mult, ALU.add))
                then(tt(nre, mag, cs, ALU.mult))
                then(V.tensor_scalar(nre, nre, 1.0, None, ALU.subtract))
                then(tt(nim, mag, sn, ALU.mult))
                then(tt(t1, nre, a_re, ALU.mult))
                then(tt(t2, nim, a_im, ALU.mult))
                then(tt(t1, t1, t2, ALU.add))
                then(tt(fre, t1, d2, ALU.mult))
                then(tt(t1, nim, a_re, ALU.mult))
                then(tt(t2, nre, a_im, ALU.mult))
                then(tt(t1, t1, t2, ALU.subtract))
                then(tt(fim, t1, d2, ALU.mult))

            def bc_source(l, n):
                dve.wait_ge(s_bc, 64 * (l + 1))
                if n < 2:
                    if n == 0:
                        then(V.memset(bsrc, 0.0))
                    else:
                        dve.wait_ge(bc_src, 4 * l + 1)
                    a, b, op = (0, 1, ALU.subtract) if n == 0 else (1, 0, ALU.add)
                    then(tt(bt[:, 0], bn[:, a], bcast(fre, GROUP), ALU.mult))
                    then(tt(bt[:, 1], bn[:, b], bcast(fim, GROUP), ALU.mult))
                    if n:
                        dve.wait_ge(bc_tr, 4 * l + 1)
                    for g in range(2):
                        p = slice(g * HEAD, (g + 1) * HEAD)
                        last = tt(bsrc[p, :, g * GROUP:(g + 1) * GROUP], bt[p, 0], bt[p, 1], op)
                else:
                    if n == 3:
                        dve.wait_ge(bc_src, 4 * l + 3)
                        dve.wait_ge(bc_tr, 4 * l + 3)
                    for g in range(2):
                        last = V.tensor_scalar(csrc[:, :, g * HEAD:(g + 1) * HEAD], cn[:, n - 2], consts[:, 4 + g:5 + g], None, ALU.mult)
                last.then_inc(bc_src, 1)

            def table(l, n):
                k = yc[:, :, :]
                if l or n:
                    dve.wait_ge(tab_sin, 4 * l + n)
                then(V.tensor_tensor(m[:, :, :], rows4(iota[:, :], 4), bcast(small[:, 9, 4 * n:4 * n + 4], T), ALU.mult))
                then(V.tensor_scalar(k, m[:, :, :], ROUND, ROUND, ALU.add, ALU.subtract))
                V.tensor_tensor(m[:, :, :], m[:, :, :], k, ALU.subtract).then_inc(tab_ang, 1)

            def mod_vectors(l, ng):
                n = 3 * l + ng
                dve.wait_ge(mod_tr, n + 1)
                c0 = 16 * ng
                V.tensor_tensor(modv[:, c0:c0 + 16].rearrange("p (q j) -> p j q", q=4), b_mod[:, 0:16].rearrange("p (j q) -> p j q", q=4),
                                vec[l][:, c0:c0 + 16].rearrange("p (q j) -> p j q", q=4), ALU.add).then_inc(mod_ready, 1)
                dve.wait_ge(mod_ready, n + 1)
                if ng != 1:
                    s, m0, r0 = (scale1, M_SC1, R_N1) if ng == 0 else (scale2, M_SC2, R_N2)
                    then(V.scalar_tensor_tensor(out=s[:, :], in0=modv[:, m0:m0 + DK], scalar=1.0, in1=vec[l][:, r0:r0 + DK], op0=ALU.add, op1=ALU.mult))

            def norm_root(n):
                dve.wait_ge(rms_ready, n + 1)
                then(V.reciprocal(rt[:, :], rt[:, :]))
                for j in range(2):
                    last = V.tensor_scalar(rinv[:, j * P:(j + 1) * P], ident[:, :], rt[:, j:j + 1], None, ALU.mult)
                last.then_inc(diag_ready, 1)
                dve.wait_ge(rinv_ready, n + 1)

            def norm(l, kind, n, s, shift):
                norm_root(n)
                h0 = H_PER_LAYER * l + H0[kind]
                for k in range(DK + 2):
                    if k < DK:
                        V.scalar_tensor_tensor(out=h[:, k, :], in0=x[:, k, :], scalar=s[:, k:k + 1], in1=b_y[:, T:2 * T],
                                               op0=ALU.mult, op1=ALU.mult).then_inc(h_ready, 1)
                    if k >= 2:
                        j = k - 2
                        dve.wait_ge(hhi_ready, h0 + j + 1)
                        V.scalar_tensor_tensor(out=hlo[:, j, :], in0=h[:, j, :], scalar=modv[:, shift + j:shift + j + 1], in1=hhi[:, j, :].bitcast(F32),
                                               op0=ALU.add, op1=ALU.subtract).then_inc(hlo_ready, 1)

            def mix_lo(l, c):
                dve.wait_ge(hhi_ready, H_PER_LAYER * l + H0["wo"] + c + 1)
                q = slice(2 * c, 2 * c + 2)
                V.tensor_tensor(hlo[:, q, :], h[:, q, :], hhi[:, q, :].bitcast(F32), ALU.subtract).then_inc(hlo_ready, 1)

            def rope(l, c):
                dve.wait_ge(rot_ready, 3 * l + c + 1)
                w = 2 if c < 2 else 1
                src = halves((b_s, b_t, b_s)[c][:, :])[:, 0:w, :]
                q = qT[:, 2 * c:2 * c + 2, :] if c < 2 else kT[:, :].rearrange("p (o t) -> p o t", o=1)
                step(V.tensor_tensor(rtmp[:, 0:w, :], src, rows4(sinr[:, :], w), ALU.mult))
                then(V.tensor_tensor(q, q, rows4(cosr[:, :], w), ALU.mult))
                V.tensor_tensor(q, q, rtmp[:, 0:w, :], ALU.add).then_inc(rope_ready, 1)
                dve.wait_ge(rope_ready, 3 * l + c + 1)

            def v_copy(l):
                dve.wait_ge(vt_ready, l + 1)
                V.tensor_copy(vv[:, :, :], b_mod[:, 0:3 * P].rearrange("p (c d) -> p c d", c=3)).then_inc(v_ready, 1)

            def softmax_max(l, r):
                n = 4 * l + r
                j, g = divmod(r, 2)
                sk = sink[:, l, 4 * g:4 * g + 4]
                b = b_s[:, :].rearrange("p (t k) -> p t k", t=4)
                dve.wait_ge(sc_ready, n + 1)
                if j == 0:
                    then(V.memset(b[0:CHUNK, :, CHUNK:KEYS], NEG))
                then(V.tensor_reduce(mx[:, :], b, AX_X, ALU.max))
                then(V.scalar_tensor_tensor(out=mx[:, :], in0=mx[:, :], scalar=HEAD ** -0.5, in1=sk, op0=ALU.mult, op1=ALU.max))
                step(V.tensor_tensor(esink[:, :], sk, mx[:, :], ALU.subtract))
                V.tensor_scalar(nmx[:, :], mx[:, :], -1.0, None, ALU.mult).then_inc(mx_ready, 1)

            def softmax_norm(l, r):
                dve.wait_ge(ex_ready, 4 * l + r + 1)
                then(V.tensor_tensor(den[:, :], den[:, :], esink[:, :], ALU.add))
                then(V.reciprocal(rden[:, :], den[:, :]))
                V.tensor_tensor(pr[:, :, :], pr[:, :, :], bcast(rden[:, :], KEYS), ALU.mult).then_inc(pr_ready, 1)

            def att_lo(l, r):
                j, g = divmod(r, 2)
                p = slice(g * HEAD, (g + 1) * HEAD)
                dve.wait_ge(at_hi, 4 * l + r + 1)
                V.tensor_tensor(blo[p, :, j * P:(j + 1) * P], b_t[p, :].rearrange("p (t q) -> p t q", t=4),
                                bhi[p, :, j * P:(j + 1) * P].bitcast(F32), ALU.subtract).then_inc(at_lo, 1)

            def ssm(l, t, i):
                n = l * ST + t
                cs, sn = rows4(ctab[:, t, :], 2), rows4(stab[:, t, :], 2)
                r = small[:, 3, t:t + 1].to_broadcast([P, T])
                pd = prod[t % 2]
                dve.wait_ge(tab_sin, 4 * (l + 1) if l else sum(j < i for j in FIRST_TABLE_AT))
                dve.wait_ge(tab_ready, 4 * l + t // 4 + 1)
                dve.wait_ge(bu_ready, n + 1)
                bu = halves(b_bu[t % 2][:, :])
                step(V.tensor_tensor(m[:, 0:2, :], bu, cs, ALU.mult))
                V.tensor_tensor(m[:, 2:4, :], bu, sn, ALU.mult).then_inc(bu_used, 1)
                dve.wait_ge(bu_used, n + 1)
                step(V.tensor_tensor(m[:, 0, :], m[:, 0, :], m[:, 3, :], ALU.add))
                step(V.tensor_tensor(m[:, 1, :], m[:, 1, :], m[:, 2, :], ALU.subtract))
                dve.wait_ge(s_dve, step.n - 1)
                step(V.tensor_tensor_scan(m[:, 0, :], r, m[:, 0, :], 0.0, ALU.mult, ALU.add))
                dve.wait_ge(s_dve, step.n - 1)
                then(V.tensor_tensor_scan(m[:, 1, :], r, m[:, 1, :], 0.0, ALU.mult, ALU.add))
                if n >= 2:
                    dve.wait_ge(y_ready, n - 1)
                V.tensor_tensor(pd[:, 0:2, :], m[:, 0:2, :], cs, ALU.mult)
                V.tensor_tensor(pd[:, 2:4, :], m[:, 0:2, :], sn, ALU.mult).then_inc(prod_ready, 1)
                dve.wait_ge(prod_ready, n + 1)

            def ssm_y(l, half):
                n = 2 * l + half
                dve.wait_ge(y_ready, 8 * (n + 1))
                for c in range(2):
                    k = 2 * half + c
                    last = V.scalar_tensor_tensor(out=ys[:, k, :], in0=u_ssm[:, k, :], scalar=vec[l][:, R_D + k:R_D + k + 1],
                                                  in1=b_y[:, c * T:(c + 1) * T], op0=ALU.mult, op1=ALU.add)
                last.then_inc(y_used, 1)

            def conv(l, pair, seg):
                for k in range(4 * seg, min(4 * seg + 4, TAPS)):
                    for c in (2 * pair, 2 * pair + 1):
                        w = tapv[l][:, c, k:k + 1]
                        if k == 0:
                            last = V.tensor_scalar(yc[:, c, :], uc[:, c, 0:T], w, vec[l][:, R_DWB + c:R_DWB + c + 1], ALU.mult, ALU.add)
                        else:
                            dve.wait_ge(s_dve, step.n - 1)
                            last = V.scalar_tensor_tensor(out=yc[:, c, :], in0=uc[:, c, k:k + T], scalar=w, in1=yc[:, c, :], op0=ALU.mult, op1=ALU.add)
                        if (k, c) == (TAPS - 1, CT - 1):
                            last.then_inc(conv_ready, 1)
                        else:
                            step(last)

            def conv_center(l):
                dve.wait_ge(mean_ready, l + 1)
                V.tensor_tensor(yc[:, :, :], yc[:, :, :], rows4(mean[:, :], 4), ALU.subtract).then_inc(cent_ready, 1)

            def conv_norm(l):
                dve.wait_ge(cstd_ready, l + 1)
                then(V.reciprocal(mean[:, :], mean[:, :]))
                V.tensor_tensor(yc[:, :, :], yc[:, :, :], rows4(mean[:, :], 4), ALU.mult).then_inc(cnorm_ready, 1)
                dve.wait_ge(c_hi, l + 1)
                V.tensor_tensor(blo[:, :, :], yc[:, :, :], bhi[:, :, :].bitcast(F32), ALU.subtract).then_inc(c_lo, 1)

            def ssm_lo(l):
                dve.wait_ge(ys_hi, l + 1)
                V.tensor_tensor(blo[:, :, :], ys[:, :, :], bhi[:, :, :].bitcast(F32), ALU.subtract).then_inc(ys_lo, 1)

            def post(l, i, parts=(0, 1)):
                kind, n = NAMES[i]
                if kind == "ca":
                    b = unit(l, i)
                    dve.wait_ge(sigb_ready, 2 * l + n + 1)
                    V.tensor_tensor(uc[:, 2 * n:2 * n + 2, PAD:PAD + T], halves(b), tmp[:, :, :], ALU.mult).then_inc(uc_ready, 1)
                    dve.wait_ge(uc_ready, 2 * l + n + 1)
                elif kind in ("ao", "cp", "gla"):
                    for half in parts:
                        c = 2 * (2 * n + half)
                        q = slice(c, c + 2)
                        v = 4 * l + 2 * n + half + 1
                        b = halves(unit(l, i, half))
                        if half == 0 and n == 0:
                            dve.wait_ge(gate_ready, 12 * l + {"ao": 4, "cp": 8, "gla": 12}[kind])
                        if kind == "ao":
                            V.tensor_tensor(h[:, q, :], b, gate[:, q, :], ALU.mult).then_inc(ao_read, 1)
                        elif kind == "cp":
                            V.tensor_tensor(tmp[:, :, :], b, gate[:, q, :], ALU.mult).then_inc(cp_read, 1)
                            dve.wait_ge(cp_read, v)
                            then(V.tensor_tensor(h[:, q, :], h[:, q, :], tmp[:, :, :], ALU.add))
                        else:
                            dve.wait_ge(glsig_ready, v)
                            V.tensor_tensor(tmp[:, :, :], b, prod[half][:, 0:2, :], ALU.mult).then_inc(gl_read, 1)
                            dve.wait_ge(gl_read, v)
                            then(V.tensor_tensor(tmp[:, :, :], tmp[:, :, :], gate[:, q, :], ALU.mult))
                            V.tensor_tensor(h[:, q, :], h[:, q, :], tmp[:, :, :], ALU.add).then_inc(h_ready, 1)
                            dve.wait_ge(h_ready, H_PER_LAYER * l + H0["wo"] + 2 * n + half + 1)
                            mix_lo(l, 2 * n + half)
                elif kind == "wo":
                    b = unit(l, i)
                    for c in range(2):
                        k = 2 * n + c
                        last = V.scalar_tensor_tensor(out=x[:, k, :], in0=b[:, c * T:(c + 1) * T], scalar=modv[:, M_G1 + k:M_G1 + k + 1],
                                                      in1=x[:, k, :], op0=ALU.mult, op1=ALU.add)
                    last.then_inc(x_mid, 1)
                elif kind == "fu":
                    b = unit(l, i)
                    a = slice(2 * (n % 2), 2 * (n % 2) + 2)
                    v = l * NF + n + 1
                    dve.wait_ge(silu_ready, v)
                    V.tensor_tensor(gate[:, a, :], halves(b), gate[:, a, :], ALU.mult).then_inc(act_ready, 1)
                    dve.wait_ge(act_hi, v)
                    V.tensor_tensor(blo[:, a, :], gate[:, a, :], bhi[:, a, :].bitcast(F32), ALU.subtract).then_inc(act_lo, 1)
                elif kind == "fo" and n == NF - 1:
                    for k in range(DK):
                        if k % 2 == 0:
                            if k < DK - 2:
                                dve.wait_ge(ffn_sum, 3 * l + k // 2 + 1)
                            else:
                                dve.wait_ge(s_unit, used(l * NB + i))
                        last = V.scalar_tensor_tensor(out=x[:, k, :], in0=bank[4 + k // 2][:, (k % 2) * T:(k % 2 + 1) * T],
                                                      scalar=modv[:, M_G2 + k:M_G2 + k + 1], in1=x[:, k, :], op0=ALU.mult, op1=ALU.add)
                        if k % 2:
                            last.then_inc(x_next, 1)
                            if l == DEPTH - 1:
                                dve.wait_ge(x_next, 4 * l + k // 2 + 1)
                                for q in (k - 1, k):
                                    V.tensor_scalar(gate[:, q, :], x[:, q, :], vec[0][:, R_FIN + q:R_FIN + q + 1], None, ALU.mult).then_inc(fin_ready, 1)

            def small_vectors_in(l):
                dve.wait_ge(s_rows[l], 16 * N_ROWS)
                V.tensor_copy(ldtr.rearrange("s (g n) -> s g n", g=2), bcast(ldt[:, :], HEAD)).then_inc(ldt_spread, 1)
                dve.wait_ge(vec_tr, l + 1)
                V.tensor_copy(vec[l][:, :], b_y[:, 0:P])
                V.tensor_copy(ldv[l][:, :], b_y[:, P:P + ST])
                V.tensor_copy(tapv[l][:, :, :], b_y[:, 256:384].rearrange("p (c k) -> p c k", c=CT)[:, :, 0:TAPS]).then_inc(vec_cp, 1)

            def side(l, t):
                if t == ROPE_Q_AT:
                    rope(l, 0)
                    rope(l, 1)
                if t == ROPE_K_AT:
                    rope(l, 2)
                    v_copy(l)
                if t - 1 in SCORES_AT:
                    softmax_norm(l, SCORES_AT[t - 1])
                if t in ATTEND_AT:
                    att_lo(l, ATTEND_AT[t])
                if t in SCORES_AT:
                    softmax_max(l, SCORES_AT[t])
                if t in SSM_Y_AT:
                    ssm_y(l, SSM_Y_AT[t])
                if t == SSM_SPLIT_AT:
                    ssm_lo(l)
                if t == CONV_MEAN_AT:
                    conv_center(l)
                if t in SSM_AT:
                    ssm(l, SSM_AT[t], t // 2)
                if t in CONV_AT:
                    conv(l, *CONV_AT[t])
                if t == CONV_VAR_AT:
                    conv_norm(l)

            small_vectors_in(0)
            dve.wait_ge(silu_c, 1)
            V.tensor_copy(cact32[:, :, :], bcast(cact[:, :], 32)).then_inc(c_ready, 1)
            discretize(0)
            b_factor(0)
            dve.wait_ge(s_const2, 16 * 5)
            then(V.tensor_copy(tmp[:, 1, :], posi))
            for n in range(4):
                bc_source(0, n)
            for mi in range(AHEAD):
                lo(mi)
            mod_vectors(0, 0)
            norm(0, "su", 0, scale1, M_SH1)
            for l in range(DEPTH):
                for i in range(NB):
                    for n in mod_ends_at(l, i - 2):
                        mod_vectors(*divmod(n, 3))
                    if i == 1:
                        then(V.memset(uc[:, :, 0:PAD], 0.0))
                    side(l, 2 * i)
                    if NAMES[i][0] in ("ao", "cp"):
                        post(l, i, (0,))
                    side(l, 2 * i + 1)
                    if (l, i) == (0, 1):
                        then(V.tensor_scalar(tmp[:, 1, :], tmp[:, 1, :], consts[:, 6:7], None, ALU.mult))
                        reduce_angle(tmp[:, 0, :], tmp[:, 1, :], rtmp[:, 0, :]).then_inc(rope_ang, 1)
                        dve.wait_ge(rope_sin, 1)
                        then(V.tensor_tensor(cosr[:, :], cosr[:, :], cosr[:, :], ALU.mult))
                        then(V.tensor_scalar(cosr[:, :], cosr[:, :], -2.0, 1.0, ALU.mult, ALU.add))
                    if l + 1 < DEPTH:
                        if i == PREP_AT - 1:
                            small_vectors_in(l + 1)
                        if i == PREP_AT:
                            discretize(l + 1)
                        if i == PREP_AT + 1:
                            b_factor(l + 1)
                        if i in BC_AT:
                            bc_source(l + 1, BC_AT[i])
                        if i in TABLE_AT:
                            table(l + 1, TABLE_AT[i])
                    if l == 0 and i in FIRST_TABLE_AT:
                        table(0, FIRST_TABLE_AT[i])
                    lo(l * NB + i + AHEAD)
                    post(l, i, (1,) if NAMES[i][0] in ("ao", "cp") else (0, 1))
                    if NAMES[i] == ("wo", 3):
                        norm(l, "fg", 2 * l + 1, scale2, M_SH2)
                if l + 1 < DEPTH:
                    norm(l + 1, "su", 2 * l + 2, scale1, M_SH1)
            dve.wait_ge(rms_ready, 2 * DEPTH + 1)
            V.reciprocal(rt[:, :], rt[:, :]).then_inc(rt_ready, 1)
            dve.wait_ge(rt_ready, 1)
            for j in range(2):
                dve.wait_ge(fin_tr, 2 * j + 2)
                V.tensor_scalar(h[:, 4 * j + 2:4 * j + 4, :], halves(bank[5 + 2 * j][:, :]), rt[:, j:j + 1], None, ALU.mult).then_inc(fin_dve, 1)


_INS = ("x", "c", "positions", "w_mod", "b_mod", "norm1_g", "w_in", "attn_sinks", "w_attn_o", "conv_dw_w", "conv_dw_b",
        "conv_ln_g", "conv_ln_b", "conv_pw_w", "ssm_a_re", "ssm_a_im", "ssm_log_dt", "ssm_b_re", "ssm_b_im", "ssm_c_re",
        "ssm_c_im", "ssm_d", "ssm_glu_a", "ssm_glu_b", "w_out", "norm2_g", "w_ffn_in", "w_ffn_out", "final_norm_g")


def constants():
    p = np.arange(P)
    small = np.zeros((P, 16), np.float32)
    small[32 * np.arange(4), np.arange(4)] = 1.0
    small[:, 4] = (p // GROUP) % 2 == 0
    small[:, 5] = (p // GROUP) % 2 == 1
    half = ROPE_DIM // 2
    inv = np.float32(THETA) ** (-np.arange(0, ROPE_DIM, 2, dtype=np.float32) / np.float32(ROPE_DIM))
    small[:, 6] = np.where(p % HEAD < ROPE_DIM, inv[p % half], 0.0)
    small[:, 7] = EPS
    rot = np.zeros((P, P), np.float32)
    for g in range(NKV):
        for j in range(half):
            rot[g * HEAD + half + j, g * HEAD + j] = -1.0
            rot[g * HEAD + j, g * HEAD + half + j] = 1.0
    iota = np.broadcast_to(np.arange(T, dtype=np.float32), (P, T))
    return {"c_ident": np.eye(P, dtype=np.float32), "c_small": small, "c_ones": np.ones((P, P), np.float32), "c_rot": rot,
            "c_iota": np.ascontiguousarray(iota)}


def kernel(**inputs):
    import concourse.bacc as _bacc
    from concourse.bass_utils import run_bass_kernel_spmd as _run

    nc = _bacc.Bacc("TRN2", target_bir_lowering=False, num_devices=1)
    arrays = {name: np.ascontiguousarray(inputs[name]) for name in _INS} | constants()
    A = {n: nc.dram_tensor(f"in_{n}", a.shape, mybir.dt.from_np(a.dtype), kind="ExternalInput").ap() for n, a in arrays.items()}
    out = nc.dram_tensor("out_0", (1, T, D), F32, kind="ExternalOutput").ap()
    trunk(nc, A, out)
    r = _run(nc, [{f"in_{n}": a for n, a in arrays.items()}], core_ids=[0])
    return r.results[0]["out_0"]
```
